# Optimizing a Trainium2 kernel written in Bass

```python
import jax, jax.numpy as jnp
from jax import lax
import numpy as np

D_MODEL = 2048
BATCH = 1
SEQ = 256
DEPTH = 2

D_MIX = D_MODEL
GLA_HEADS = 6
GLA_DK = 64
GLA_DV = 128
GLA_GATE_RANK = 16
GLA_GATE_TEMP = 16.0
GLA_CHUNK = 64
GLA_WIDTH = GLA_HEADS * GLA_DV
MLA_HEADS = 6
MLA_Q_LORA = 384
MLA_KV_LORA = 256
MLA_NOPE = 128
MLA_ROPE = 64
MLA_DV = 128
MLA_WIDTH = MLA_HEADS * MLA_DV
ROPE_THETA = 10000.0
Q_BLOCK = 128
CONV_CH = D_MIX - GLA_WIDTH - MLA_WIDTH
CONV_K = 3
EPS = 1e-6

IN_SPLIT_SIZES = (
    GLA_HEADS * GLA_DK,
    GLA_HEADS * GLA_DK,
    GLA_WIDTH,
    2 * GLA_GATE_RANK,
    MLA_Q_LORA,
    MLA_KV_LORA,
    MLA_ROPE,
    CONV_CH,
    CONV_CH,
    CONV_CH,
    D_MIX,
)
IN_DIM = sum(IN_SPLIT_SIZES)

kernel_name = "bidir_hybrid_gla_mla_shortconv_adaln"

def rms_norm(x, g):
    xf = x.astype(jnp.float32)
    y = xf * lax.rsqrt(jnp.mean(xf * xf, axis=-1, keepdims=True) + EPS)
    return (y * g.astype(jnp.float32)).astype(x.dtype)

def rope(x, cos, sin):
    x1, x2 = jnp.split(x.astype(jnp.float32), 2, axis=-1)
    out = jnp.concatenate([x1 * cos - x2 * sin, x2 * cos + x1 * sin], axis=-1)
    return out.astype(x.dtype)

def gla_chunked(q, k, v, log_a, strict):
    bsz, s, h, dk = q.shape
    dv = v.shape[-1]
    n = s // GLA_CHUNK

    def to_chunks(t):
        return t.reshape(bsz, n, GLA_CHUNK, h, t.shape[-1]).transpose(0, 3, 1, 2, 4).astype(jnp.float32)

    q, k, v, g = to_chunks(q), to_chunks(k), to_chunks(v), to_chunks(log_a)
    b = jnp.cumsum(g, axis=3)
    b_last = b[:, :, :, -1:, :]
    q_dec = q * jnp.exp(b)
    k_inv = k * jnp.exp(-b)
    k_to_end = k * jnp.exp(b_last - b)
    scores = jnp.einsum('bhncd,bhnjd->bhncj', q_dec, k_inv)
    mask = jnp.tril(jnp.ones((GLA_CHUNK, GLA_CHUNK), dtype=bool), k=-1 if strict else 0)
    o_intra = jnp.einsum('bhncj,bhnje->bhnce', jnp.where(mask, scores, 0.0), v)
    chunk_kv = jnp.einsum('bhncd,bhnce->bhnde', k_to_end, v)
    chunk_decay = jnp.exp(b_last[:, :, :, 0, :])

    def step(state, inp):
        decay, kv = inp
        return decay[..., None] * state + kv, state

    init = jnp.zeros((bsz, h, dk, dv), jnp.float32)
    _, s_before = lax.scan(step, init, (jnp.moveaxis(chunk_decay, 2, 0), jnp.moveaxis(chunk_kv, 2, 0)))
    s_before = jnp.moveaxis(s_before, 0, 2)
    o = o_intra + jnp.einsum('bhncd,bhnde->bhnce', q_dec, s_before)
    return o.transpose(0, 2, 3, 1, 4).reshape(bsz, s, h, dv)

def mla_attention(q_nope, q_rope, k_nope, k_rope, v):
    bsz, s, h, _ = q_nope.shape
    nb = s // Q_BLOCK
    scale = (MLA_NOPE + MLA_ROPE) ** -0.5

    def blocks(t):
        return t.reshape(bsz, nb, Q_BLOCK, *t.shape[2:]).swapaxes(0, 1)

    def attend(qb):
        qn, qr = qb
        sc = jnp.einsum('bqhd,bkhd->bhqk', qn, k_nope) + jnp.einsum('bqhr,bkr->bhqk', qr, k_rope)
        p = jax.nn.softmax(sc.astype(jnp.float32) * scale, axis=-1).astype(v.dtype)
        return jnp.einsum('bhqk,bkhd->bqhd', p, v)

    o = lax.map(attend, (blocks(q_nope), blocks(q_rope)))
    return o.swapaxes(0, 1).reshape(bsz, s, h * v.shape[-1])

def hybrid_layer(x, c_act, cos, sin, ada_w, ada_b, norm_g, w_in,
                 gla_wg_f, gla_bg_f, gla_wg_b, gla_bg_b, gla_norm_g,
                 mla_q_norm_g, mla_kv_norm_g, mla_w_uq, mla_w_ukv, mla_out_g,
                 conv_w, conv_out_g, w_out):
    bsz, s, _ = x.shape
    shift, scale, gate = jnp.split(c_act @ ada_w + ada_b, 3, axis=-1)
    h = rms_norm(x, norm_g) * (1.0 + scale[:, None, :]) + shift[:, None, :]
    proj = h @ w_in
    split_idx = [int(i) for i in np.cumsum(IN_SPLIT_SIZES)[:-1]]
    (gq, gk, gv, g_lr, mq, mkv, mkr, cb, cc, cx, z) = jnp.split(proj, split_idx, axis=-1)

    q = gq.reshape(bsz, s, GLA_HEADS, GLA_DK) * (GLA_DK ** -0.5)
    k = gk.reshape(bsz, s, GLA_HEADS, GLA_DK)
    v = gv.reshape(bsz, s, GLA_HEADS, GLA_DV)
    lr_f, lr_b = jnp.split(g_lr, 2, axis=-1)
    la_f = jax.nn.log_sigmoid((lr_f @ gla_wg_f + gla_bg_f).astype(jnp.float32)) / GLA_GATE_TEMP
    la_b = jax.nn.log_sigmoid((lr_b @ gla_wg_b + gla_bg_b).astype(jnp.float32)) / GLA_GATE_TEMP
    la_f = la_f.reshape(bsz, s, GLA_HEADS, GLA_DK)
    la_b = la_b.reshape(bsz, s, GLA_HEADS, GLA_DK)
    o_fwd = gla_chunked(q, k, v, la_f, strict=False)
    o_bwd = jnp.flip(gla_chunked(jnp.flip(q, 1), jnp.flip(k, 1), jnp.flip(v, 1), jnp.flip(la_b, 1), strict=True), 1)
    o_gla = rms_norm((o_fwd + o_bwd).astype(x.dtype), gla_norm_g).reshape(bsz, s, GLA_WIDTH)

    cq = rms_norm(mq, mla_q_norm_g)
    qm = (cq @ mla_w_uq).reshape(bsz, s, MLA_HEADS, MLA_NOPE + MLA_ROPE)
    q_nope, q_rope = qm[..., :MLA_NOPE], rope(qm[..., MLA_NOPE:], cos[:, :, None, :], sin[:, :, None, :])
    ckv = rms_norm(mkv, mla_kv_norm_g)
    kv = (ckv @ mla_w_ukv).reshape(bsz, s, MLA_HEADS, MLA_NOPE + MLA_DV)
    k_nope, v_m = kv[..., :MLA_NOPE], kv[..., MLA_NOPE:]
    k_rope = rope(mkr, cos, sin)
    o_mla = rms_norm(mla_attention(q_nope, q_rope, k_nope, k_rope, v_m), mla_out_g)

    u = cc * cx
    up = jnp.pad(u, ((0, 0), (1, 1), (0, 0)))
    conv = up[:, :-2] * conv_w[0] + up[:, 1:-1] * conv_w[1] + up[:, 2:] * conv_w[2]
    o_conv = rms_norm(cb * conv, conv_out_g)

    y = jnp.concatenate([o_gla, o_mla, o_conv], axis=-1) * jax.nn.silu(z)
    return x + gate[:, None, :] * (y @ w_out)

def setup_inputs(seed: int = 0) -> dict:
    key = jax.random.key(seed)
    ks = jax.random.split(key, 24)
    f32 = jnp.float32

    def nrm(k, shape, std):
        return std * jax.random.normal(k, shape, f32)

    def gain(k, shape):
        return 1.0 + 0.1 * jax.random.normal(k, shape, f32)

    L = DEPTH
    offsets = jax.random.randint(ks[2], (BATCH, 1), 0, 1024, dtype=jnp.int32)
    positions = offsets + jnp.arange(SEQ, dtype=jnp.int32)[None, :]
    return {
        "x": nrm(ks[0], (BATCH, SEQ, D_MODEL), 1.0),
        "c": nrm(ks[1], (BATCH, D_MODEL), 1.0),
        "positions": positions,
        "ada_w": nrm(ks[3], (L, D_MODEL, 3 * D_MODEL), 0.5 * D_MODEL ** -0.5),
        "ada_b": nrm(ks[4], (L, 3 * D_MODEL), 0.02),
        "norm_g": gain(ks[5], (L, D_MODEL)),
        "w_in": nrm(ks[6], (L, D_MODEL, IN_DIM), D_MODEL ** -0.5),
        "gla_wg_f": nrm(ks[7], (L, GLA_GATE_RANK, GLA_HEADS * GLA_DK), GLA_GATE_RANK ** -0.5),
        "gla_bg_f": nrm(ks[8], (L, GLA_HEADS * GLA_DK), 0.1),
        "gla_wg_b": nrm(ks[9], (L, GLA_GATE_RANK, GLA_HEADS * GLA_DK), GLA_GATE_RANK ** -0.5),
        "gla_bg_b": nrm(ks[10], (L, GLA_HEADS * GLA_DK), 0.1),
        "gla_norm_g": gain(ks[11], (L, GLA_DV)),
        "mla_q_norm_g": gain(ks[12], (L, MLA_Q_LORA)),
        "mla_kv_norm_g": gain(ks[13], (L, MLA_KV_LORA)),
        "mla_w_uq": nrm(ks[14], (L, MLA_Q_LORA, MLA_HEADS * (MLA_NOPE + MLA_ROPE)), MLA_Q_LORA ** -0.5),
        "mla_w_ukv": nrm(ks[15], (L, MLA_KV_LORA, MLA_HEADS * (MLA_NOPE + MLA_DV)), MLA_KV_LORA ** -0.5),
        "mla_out_g": gain(ks[16], (L, MLA_WIDTH)),
        "conv_w": nrm(ks[17], (L, CONV_K, CONV_CH), CONV_K ** -0.5),
        "conv_out_g": gain(ks[18], (L, CONV_CH)),
        "w_out": nrm(ks[19], (L, D_MIX, D_MODEL), D_MIX ** -0.5),
        "final_g": gain(ks[20], (D_MODEL,)),
    }

def reference(x, c, positions, ada_w, ada_b, norm_g, w_in,
              gla_wg_f, gla_bg_f, gla_wg_b, gla_bg_b, gla_norm_g,
              mla_q_norm_g, mla_kv_norm_g, mla_w_uq, mla_w_ukv, mla_out_g,
              conv_w, conv_out_g, w_out, final_g):
    inv_freq = ROPE_THETA ** (-jnp.arange(0, MLA_ROPE, 2, dtype=jnp.float32) / MLA_ROPE)
    ang = positions.astype(jnp.float32)[..., None] * inv_freq
    cos, sin = jnp.cos(ang), jnp.sin(ang)
    c_act = jax.nn.silu(c)
    h = x
    for l in range(DEPTH):
        h = hybrid_layer(h, c_act, cos, sin, ada_w[l], ada_b[l], norm_g[l], w_in[l],
                         gla_wg_f[l], gla_bg_f[l], gla_wg_b[l], gla_bg_b[l], gla_norm_g[l],
                         mla_q_norm_g[l], mla_kv_norm_g[l], mla_w_uq[l], mla_w_ukv[l], mla_out_g[l],
                         conv_w[l], conv_out_g[l], w_out[l])
    return rms_norm(h, final_g)


_drawn_inputs = setup_inputs


def setup_inputs(seed=0):
    import zlib

    import numpy as np

    out = dict(_drawn_inputs(seed))
    spreads = {}
    factors = {'gla_bg_f': 8.0,
     'gla_bg_b': 8.0,
     'gla_norm_g': 3.239,
     'mla_q_norm_g': 8.0,
     'mla_kv_norm_g': 3.119,
     'mla_out_g': 3.348,
     'conv_out_g': 3.967}
    for name, (base, spread) in spreads.items():
        noise = np.random.default_rng([zlib.crc32(name.encode()), seed]).standard_normal(out[name].shape)
        drawn = base * np.exp(spread * noise) if base else spread * noise
        out[name] = __import__('jax').numpy.asarray(drawn.astype(out[name].dtype))
    for name, factor in factors.items():
        out[name] = (out[name] * factor).astype(out[name].dtype)
    return out
```

```python
from contextlib import ExitStack

import concourse.bass as bass
from concourse import mybir

P = 128
D = 2048
T = 256
DEPTH = 2
KT = D // P
HEADS = 6
PAIRS = HEADS // 2
DK = 64
CH = 64
NCH = T // CH
RANK = 16
QL, KVL = 384, 256
CONVT = 4
EPS = 1e-6
ROWS = 4
RING, SPLIT = 5, 2
WIDE = 512
ADA_GROUPS = 3 * D // WIDE
SM_SCALE = (128 + 64) ** -0.5

GROUPS = (
    [("latq", 512, ROWS, 4), ("latkv", 512, ROWS, 4), ("gq", 384, ROWS, 4), ("gk", 384, ROWS, 4)]
    + [(f"uq{i}", 512, 3, 1) for i in range(3)]
    + [(f"kn{i}", 384, 2, 1) for i in range(2)]
    + [(f"vm{i}", 384, 2, 1) for i in range(2)]
    + [(f"gv{i}", 384, ROWS, 4) for i in range(2)]
    + [(f"conv{i}", 384, ROWS, 4) for i in range(CONVT)]
    + [(f"z{i}", 512, ROWS, 4) for i in range(4)]
    + [(f"out{i}", 512, ROWS, 4) for i in range(4)]
)
GROUP_AT = {g[0]: n for n, g in enumerate(GROUPS)}
NG = len(GROUPS)
CHUNKS = [(n, k) for n, g in enumerate(GROUPS) for k in range(g[3])]
NC = len(CHUNKS)
FIRST_CHUNK = {g: min(i for i, (n, _) in enumerate(CHUNKS) if GROUPS[n][0] == g) for g in GROUP_AT}
LAST_CHUNK = {g: max(i for i, (n, _) in enumerate(CHUNKS) if GROUPS[n][0] == g) for g in GROUP_AT}
SIZES = [P * GROUPS[n][1] * GROUPS[n][2] for n, _ in CHUNKS]
STREAM_AT = [sum(SIZES[:i]) for i in range(NC + 1)]
Y_ORDER = [12, 13, 14, 15, 8, 9, 10, 11, 4, 5, 6, 7, 0, 1, 2, 3]

C_NORM, C_ADAB, C_BGF, C_BGB, C_GLAG, C_QG, C_KVG, C_MLAG, C_CW, C_CG = (
    0, 16, 64, 67, 70, 71, 74, 76, 82, 94)
SMALL = 98
K_ONES, K_ID, K_MF, K_MB, K_SCAN, K_SEL, K_SIGN, K_FREQ, K_EPS = 0, 128, 256, 512, 768, 1024, 1025, 1026, 1027
CONST = 1028

MLA_AT = LAST_CHUNK["vm1"] + 2
GLA_AT = MLA_AT + HEADS + 3
GLA_STEPS = 5
MLAN_AT = GLA_AT + 1
GLAN_AT = GLA_AT + GLA_STEPS * PAIRS
CONVN_AT = GLAN_AT + PAIRS
MAGIC = 1.5 * 2.0 ** 23
TWO_PI = (6.28125, 2029 / 2.0 ** 20, 6.283185307179586 - 6.28125 - 2029 / 2.0 ** 20)


def ada_plan(layer):
    now = [(layer, g) for g in range(8, 12)]
    after = [(layer + 1, g) for g in range(8)] if layer + 1 < DEPTH else []
    return now + after


def ada_before(layer, c):
    total = 4 * len(ada_plan(layer))
    return min(total, max(0, total * c // (NC - 6)))


ADA_FIRST = [8 * 4]
for _l in range(DEPTH):
    ADA_FIRST.append(ADA_FIRST[-1] + 4 * len(ada_plan(_l)))
LOADS = [("a", n) for n in range(ADA_FIRST[0])]
for _l in range(DEPTH):
    for _c in range(NC):
        LOADS += [("a", ADA_FIRST[_l] + n) for n in range(ada_before(_l, _c - 1), ada_before(_l, _c))]
        LOADS.append(("w", _l * NC + _c))
PLACE = {key: i for i, key in enumerate(LOADS)}


def build(nc, xT, cT, posr, wstream, adastream, wg, small, finalg, const, out):
    F32, F32R, I32 = mybir.dt.float32, mybir.dt.float32r, mybir.dt.int32
    ALU, ACT, AX = mybir.AluOpType, mybir.ActivationFunctionType, mybir.AxisListType
    with ExitStack() as ctx:
        def sb(name, shape, dt=F32):
            return ctx.enter_context(nc.sbuf_tensor(name, shape, dt))

        def bank(name):
            return ctx.enter_context(nc.psum_tensor(name, [P, 512], F32))

        sems = {}

        def sem(name):
            if name not in sems:
                sems[name] = ctx.enter_context(nc.semaphore(name))
            return sems[name]

        x = sb("x", [P, KT, T])
        a_hi = sb("a_hi", [P, KT, T], F32R)
        a_lo = sb("a_lo", [P, KT, T], F32R)
        o = sb("o", [P, KT, T])
        ring = sb("ring", [P, RING, ROWS * WIDE])
        w_hi = sb("w_hi", [P, SPLIT, ROWS * WIDE], F32R)
        w_lo = sb("w_lo", [P, SPLIT, ROWS * WIDE], F32R)
        arow = sb("arow", [P, WIDE])
        acol = sb("acol", [P, DEPTH, 48])
        hscale = sb("hscale", [P, KT])
        ct = sb("ct", [P, KT])
        cz = sb("cz", [P, KT, 32])
        kst = sb("kst", [P, CONST])
        par = sb("par", [P, DEPTH, SMALL])
        fing = sb("fing", [P, KT])
        wgs = sb("wgs", [64, DEPTH, 2 * QL])
        pos_i = sb("pos_i", [P, T], I32)
        rope_cos = sb("rope_cos", [P, T])
        rope_sin = sb("rope_sin", [P, T])
        sqx = sb("sqx", [P, 4, T])
        sqo = sb("sqo", [P, 4, T])
        rs = sb("rs", [P, 2 * T])
        rinv = sb("rinv", [P, 2 * T])
        tmp = sb("tmp", [P, 4, T])
        gx = tmp[:, 0:2, :].rearrange("p a b -> p (a b)")
        gt = tmp[:, 2:4, :].rearrange("p a b -> p (a b)")
        sz = tmp[:, :, :].rearrange("p (j a) b -> p j (a b)", j=2)
        lat = sb("lat", [P, HEADS, T])
        kn = lat
        lat_hi = sb("lat_hi", [P, 5, T], F32R)
        lat_lo = sb("lat_lo", [P, 5, T], F32R)
        kr = sb("kr", [P, T])
        qr = sb("qr", [P, PAIRS, T])
        cv = sb("cv", [P, 2, T])
        ropet = cv
        mx = sb("mx", [P, 2])
        nmx = sb("nmx", [P, 2])
        rsum = sb("rsum", [P, 2])
        rsi = sb("rsi", [P, 2])
        lrT = sb("lrT", [64, T])
        e_q = sb("e_q", [P, 2, T])
        e_k = sb("e_k", [P, 2, T])
        prob, probT = e_q, e_k[:, :, :].rearrange("p a b -> p (a b)")
        vm = sb("vm", [P, 2, HEADS * P])
        gla = vm[:, :, :].rearrange("p a b -> p (a b)")
        cs = gla[:, 0:2 * T]
        e_e = gla[:, 2 * T:4 * T].rearrange("p (a b) -> p a b", a=2)
        keT = gla[:, 4 * T:6 * T].rearrange("p (a b) -> p a b", a=4)
        ang, turns = cs, gx
        dec = sb("dec", [P, 2, NCH])
        gv = sb("gv", [P, 2, HEADS * P])
        st = sb("st", [P, 2, 2, P])
        sta = sb("sta", [P, 2, 3, P])
        ccs = sb("ccs", [P, T])
        u = sb("u", [P, T + 2])

        pp = [bank(f"pp{i}") for i in range(4)]
        pa, ps, pt, pn = bank("pa"), bank("ps"), bank("pt"), bank("pn")

        ones, ident = kst[:, K_ONES:K_ONES + P], kst[:, K_ID:K_ID + P]
        eps = kst[:, K_EPS:K_EPS + 1]

        def chunk_no(l, c):
            return l * NC + c

        def gbanks(n):
            return pp[2 * (n % 2)], pp[2 * (n % 2) + 1]

        def tile_of(n, j):
            return gbanks(n)[j // 2][:, (j % 2) * T:(j % 2) * T + T]

        def p(l, col, n=1):
            return par[:, l, col:col + n]

        ADA = [(l, g, k) for l, g in [(0, g) for g in range(8)] + [q for l in range(DEPTH) for q in ada_plan(l)]
               for k in range(4)]

        def slot(kind, n):
            return PLACE[kind, n] % RING

        def landed(eng, kind, n):
            i = PLACE[kind, n]
            eng.wait_ge(sem(f"ring_in{i % RING}"), 16 * (i // RING + 1))

        block = ctx.enter_context(nc.Block())

        @block.sync
        def _(sp):
            sp.dma_start(ct[:, :], cT).then_inc(sem("c_in"), 16)
            sp.dma_start(kst[:, :], const).then_inc(sem("const_in"), 16)
            sp.dma_start(pos_i[:, :], posr.partition_broadcast(P)).then_inc(sem("pos_in"), 16)
            sp.dma_start(par[:, :, :], small).then_inc(sem("par_in"), 16)
            sp.dma_start(x[:, :, :], xT).then_inc(sem("x_in"), 16)

            for i, (kind, n) in enumerate(LOADS):
                if i >= RING:
                    before, m = LOADS[i - RING]
                    if before == "a":
                        sp.wait_ge(sem("ada_used"), m + 1)
                    else:
                        sp.wait_ge(sem("lo_ready"), m + 1)
                if kind == "a":
                    l, g, k = ADA[n]
                    src, cols = adastream[l, g, k], ROWS * WIDE
                else:
                    l, c = divmod(n, NC)
                    cols = GROUPS[CHUNKS[c][0]][1] * GROUPS[CHUNKS[c][0]][2]
                    src = wstream[l, STREAM_AT[c]:STREAM_AT[c + 1]].rearrange("(p n) -> p n", p=P)
                sp.dma_start(ring[:, i % RING, 0:cols], src).then_inc(sem(f"ring_in{i % RING}"), 16)
                if i == 0:
                    sp.dma_start(wgs[:, :, :], wg).then_inc(sem("wg_in"), 16)
                    sp.dma_start(fing[:, :], finalg).then_inc(sem("fin_in"), 16)
            for t in range(KT):
                sp.wait_ge(sem("final_ready"), t + 1)
                sp.dma_start(out[:, t, :], o[:, t, :]).then_inc(sem("out_done"), 16)
            sp.wait_ge(sem("out_done"), 16 * KT)

        @block.gpsimd
        def _(pool):
            pool.memset(cz[:, :, :], 0.0).then_inc(sem("cz_zero"), 1)
            pool.memset(st[:, :, :, :], 0.0).then_inc(sem("st_zero"), 1)
            pool.memset(u[:, :], 0.0).then_inc(sem("u_zero"), 1)

            def squares(tiles, ready, first):
                for i, t in enumerate(tiles):
                    n = first + i
                    if n >= 4:
                        pool.wait_ge(sem("osq_used"), n - 3)
                    pool.wait_ge(*ready(i))
                    pool.tensor_tensor(sqo[:, n % 4, :], o[:, t, :], o[:, t, :], ALU.mult
                                       ).then_inc(sem("osq_ready"), 1)

            def gate_z(l, i):
                for j in range(2):
                    pool.wait_ge(sem("silu_ready"), 8 * l + 2 * i + j + 1)
                    t = Y_ORDER[4 * i + 2 * j]
                    if i == 0:
                        pool.wait_ge(sem("onorm_conv"), 4 * (l + 1))
                    else:
                        pool.wait_ge(sem("onorm_mla"), 6 * (l + 1))
                        pool.wait_ge(sem("onorm_gla"), 3 * (l + 1))
                    pool.tensor_tensor(o[:, t:t + 2, :], o[:, t:t + 2, :],
                                       sz[:, j, :].rearrange("p (a b) -> p a b", a=2), ALU.mult
                                       ).then_inc(sem("y_ready"), 1)

            for l in range(DEPTH):
                squares(range(6, 12), lambda i: (sem("o_mla"), 6 * l + i + 1), 16 * l)
                squares(range(0, 6), lambda i: (sem("o_gla"), 6 * l + i + 1), 16 * l + 6)
                squares(range(12, 16), lambda i: (sem("o_conv"), 4 * l + i + 1), 16 * l + 12)
                for i in range(4):
                    gate_z(l, i)

        @block.scalar
        def _(act):
            A = act.activation

            def split_hi(n):
                g, _ = CHUNKS[n % NC]
                cols = GROUPS[g][1] * GROUPS[g][2]
                landed(act, "w", n)
                if n >= SPLIT:
                    act.wait_ge(sem("chunk_done"), n - SPLIT + 1)
                A(w_hi[:, n % SPLIT, 0:cols], ring[:, slot("w", n), 0:cols], ACT.Identity
                  ).then_inc(sem("hi_ready"), 1)

            def ada_rows(m):
                act.wait_ge(sem("ada_used"), 4 * m + 4)
                if m >= 1:
                    act.wait_ge(sem("ada_turned"), m)
                A(arow[:, :], pa[:, :], ACT.Identity).then_inc(sem("arow_ready"), 1)

            def root(psum, lo, hi, width, norms_before):
                if norms_before:
                    act.wait_ge(sem("rinv_ready"), norms_before)
                A(rs[:, lo:hi], psum, ACT.Sqrt, bias=eps, scale=1.0 / width).then_inc(sem("root_ready"), 1)

            def h_hi(l, t):
                act.wait_ge(sem("hmul_ready"), 16 * l + t + 1)
                if t == 0 and l > 0:
                    act.wait_ge(sem("chunk_done"), chunk_no(l, 0))
                A(a_hi[:, t, :], tmp[:, t % 4, :], ACT.Identity, bias=acol[:, l, t:t + 1]
                  ).then_inc(sem("ahi_ready"), 1)

            def square_x(m):
                if m >= 16:
                    act.wait_ge(sem("x_ready"), m - 15)
                if m >= 4:
                    act.wait_ge(sem("xsq_used"), m - 3)
                A(sqx[:, m % 4, :], x[:, m % 16, :], ACT.Square).then_inc(sem("xsq_ready"), 1)

            def copy(dst, src, done):
                A(dst, src, ACT.Identity).then_inc(sem(done), 1)

            act.wait_ge(sem("c_in"), 16)
            act.wait_ge(sem("cz_zero"), 1)
            A(cz[:, :, 0], ct[:, :], ACT.Silu).then_inc(sem("cz_ready"), 1)
            act.wait_ge(sem("angle_ready"), 2)
            A(rope_cos[:, :], ang[:, 0:T], ACT.Sin).then_inc(sem("trig"), 1)
            A(rope_sin[:, :], ang[:, T:2 * T], ACT.Sin).then_inc(sem("trig"), 1)
            act.wait_ge(sem("x_in"), 16)
            act.wait_ge(sem("const_in"), 16)
            for m in range(16):
                square_x(m)
            act.wait_ge(sem("xsq_used"), 16)
            root(ps[:, 0:T], 0, T, D, 0)
            for m in range(8):
                ada_rows(m)
            split_hi(0)

            for l in range(DEPTH):
                for t in range(KT):
                    h_hi(l, t)
                for c, (g, k) in enumerate(CHUNKS):
                    n = chunk_no(l, c)
                    if n + 1 < DEPTH * NC:
                        split_hi(n + 1)
                    name = GROUPS[g][0]
                    gn = l * NG + g
                    i = int(name[-1]) if name[-1].isdigit() else 0
                    if k == GROUPS[g][3] - 1:
                        b0, b1 = gbanks(gn)
                        act.wait_ge(sem("chunk_done"), n + 1)
                        if name == "latq":
                            copy(lrT[:, :], b0[0:64, 0:T], "lr_ready")
                            copy(lat[:, 0, :], b0[:, T:2 * T], "lat_ready")
                            copy(lat[:, 1:3, :], b1[:, :].rearrange("p (a b) -> p a b", a=2), "lat_ready")
                        elif name == "latkv":
                            copy(lat[:, 3:5, :], b0[:, :].rearrange("p (a b) -> p a b", a=2), "lat_ready")
                            act.wait_ge(sem("lat_ready"), 3 * (l + 1))
                            for i in range(5):
                                if i == 4:
                                    act.wait_ge(sem("latsq_used"), 5 * l + 1)
                                A(sqx[:, i % 4, :], lat[:, i, :], ACT.Square).then_inc(sem("latsq_ready"), 1)
                            act.wait_ge(sem("latsq_used"), 5 * l + 5)
                            root(pn[:, 0:T], 0, T, QL, 7 * l + 1)
                            root(pn[:, T:2 * T], T, 2 * T, KVL, 7 * l + 1)
                            for i in range(5):
                                act.wait_ge(sem("latn_ready"), 5 * l + i + 1)
                                copy(lat_hi[:, i, :], lat[:, i, :], "lathi_ready")
                        elif name in ("gq", "gk"):
                            for i in range(3):
                                copy(o[:, 2 * i + (name == "gk"), :], tile_of(gn, i), "gqk_ready")
                        elif name[:2] == "uq":
                            act.wait_ge(sem("rope_used"), 4 * l + i + 2)
                            copy(o[:, 6 + 2 * i, :], tile_of(gn, 0), "qn_ready")
                            copy(o[:, 7 + 2 * i, :], tile_of(gn, 3), "qn_ready")
                        elif name[:2] == "kn":
                            for j in range(3):
                                copy(kn[:, 3 * i + j, :], tile_of(gn, j), "kn_ready")
                        elif name[:2] in ("vm", "gv"):
                            dst, done = (vm, "vm_ready") if name[:2] == "vm" else (gv, "gv_ready")
                            for j in range(2):
                                copy(dst[:, j, 384 * i:384 * i + 384], (b0, b1)[j][:, 0:384], done)
                        elif name[:4] == "conv":
                            if i + l > 0:
                                act.wait_ge(sem("u_ready"), 4 * l + i)
                            copy(ccs[:, :], b0[:, 0:T], "cc_ready")
                        elif name[0] == "z":
                            for j in range(2):
                                m = 8 * l + 2 * i + j
                                if m >= 2:
                                    act.wait_ge(sem("y_ready"), m - 1)
                                A(sz[:, j, :], (b0, b1)[j][:, :], ACT.Silu).then_inc(sem("silu_ready"), 1)
                    h = c - MLA_AT - 2
                    if 0 <= h < HEADS:
                        act.wait_ge(sem("pv_done"), HEADS * l + h + 1)
                        copy(o[:, 6 + h, :], pn[:, 0:T], "o_mla")
                    h = c - MLA_AT - 1
                    if 0 <= h < HEADS:
                        act.wait_ge(sem("prob_used"), HEADS * l + h + 1)
                        if l + h > 0:
                            act.wait_ge(sem("pv_done"), HEADS * l + h)
                        copy(probT[:, :], pt[:, :], "probT_ready")
                    h = c - MLA_AT
                    if 0 <= h < HEADS:
                        act.wait_ge(sem("nmx_ready"), HEADS * l + h + 1)
                        if l + h > 0:
                            act.wait_ge(sem("prob_used"), HEADS * l + h)
                        for q in range(2):
                            A(prob[:, q, :], ps[:, q * T:q * T + T], ACT.Exp, bias=nmx[:, q:q + 1],
                              scale=SM_SCALE, accum_out=rsum[:, q:q + 1]).then_inc(sem("exp_ready"), 1)
                    for pr in range(PAIRS):
                        s0 = GLA_AT + GLA_STEPS * pr
                        m = PAIRS * l + pr
                        if c == s0:
                            act.wait_ge(sem("gx_ready"), 2 * m + 2)
                            A(gt[:, :], gx[:, :], ACT.Abs).then_inc(sem("abs_ready"), 1)
                            act.wait_ge(sem("abs_ready"), m + 1)
                            A(gt[:, :], gt[:, :], ACT.Exp, scale=-1.0).then_inc(sem("eabs_ready"), 1)
                            act.wait_ge(sem("eabs_ready"), m + 1)
                            A(gt[:, :], gt[:, :], ACT.Ln, bias=1.0).then_inc(sem("ln_ready"), 1)
                            act.wait_ge(sem("cs_ready"), 2 * m + 2)
                            if m > 0:
                                act.wait_ge(sem("pair_done"), m)
                            both = cs[:, :].rearrange("p (a b) -> p a b", a=2)
                            A(e_q[:, :, :], both, ACT.Exp, scale=1 / 16).then_inc(sem("expb_ready"), 1)
                            A(e_k[:, :, :], both, ACT.Exp, scale=-1 / 16).then_inc(sem("expb_ready"), 1)
                            act.wait_ge(sem("bdiff_ready"), 2 * m + 2)
                            A(e_e[:, :, :], e_e[:, :, :], ACT.Exp, scale=1 / 16).then_inc(sem("expe_ready"), 1)
                        if c == s0 + 2:
                            act.wait_ge(sem("keT_psum"), m + 1)
                            if m > 0:
                                act.wait_ge(sem("kv_done"), m)
                            copy(keT[:, :, :], pt[:, :].rearrange("p (a b) -> p a b", a=4), "keT_ready")
                        if c == s0 + 4:
                            act.wait_ge(sem("pair_done"), m + 1)
                            copy(o[:, 2 * pr, :], pn[:, 0:T], "o_gla")
                            copy(o[:, 2 * pr + 1, :], ps[:, 0:T], "o_gla")
                    if c == MLAN_AT:
                        act.wait_ge(sem("osq_used"), 16 * l + 6)
                        root(pn[:, 0:T], 0, T, HEADS * P, 7 * l + 2)
                    for pr in range(PAIRS):
                        if c == GLAN_AT + pr:
                            act.wait_ge(sem("osq_used"), 16 * l + 8 + 2 * pr)
                            root((pt, ps, pt)[pr][:, :], 0, 2 * T, P, 7 * l + 3 + pr)
                    if c == CONVN_AT:
                        act.wait_ge(sem("osq_used"), 16 * l + 16)
                        root(pn[:, 0:T], 0, T, CONVT * P, 7 * l + 6)
                    if c == LAST_CHUNK["z3"]:
                        for t in range(KT):
                            act.wait_ge(sem("y_ready"), 8 * l + t // 2 + 1)
                            copy(a_hi[:, t, :], o[:, Y_ORDER[t], :], "yhi_ready")
                    if name[:3] == "out" and k == 3:
                        for j in range(4):
                            square_x(16 * (l + 1) + 4 * i + j)
                    for m in range(ada_before(l, c) // 4, ada_before(l, c + 1) // 4):
                        ada_rows(ADA_FIRST[l] // 4 + m)
                act.wait_ge(sem("xsq_used"), 16 * (l + 2))
                root(ps[:, 0:T], 0, T, D, 7 * (l + 1))

        @block.tensor
        def _(pe):
            def ada_chunk(n):
                l, g, k = ADA[n]
                landed(pe, "a", n)
                if k == 0 and n >= 4:
                    pe.wait_ge(sem("ada_biased"), n // 4)
                for r in range(ROWS):
                    mm = pe.matmul(pa[32 * r:32 * r + 32, :], cz[:, ROWS * k + r, :],
                                   ring[:, slot("a", n), r * WIDE:(r + 1) * WIDE],
                                   start=(k == 0), stop=(k == 3))
                mm.then_inc(sem("ada_used"), 1)

            def ada_turn(m):
                pe.wait_ge(sem("arow_ready"), m + 1)
                for j in range(4):
                    mm = pe.matmul(pa[:, j:j + 1], arow[:, j * P:(j + 1) * P], kst[:, K_SEL:K_SEL + 1],
                                   start=True, stop=True)
                mm.then_inc(sem("ada_turned"), 1)

            def xsum(m):
                pe.wait_ge(sem("xsq_ready"), m + 1)
                mm = pe.matmul(ps[:, 0:T], ones, sqx[:, m % 4, :], start=(m % 16 == 0), stop=(m % 16 == 15))
                mm.then_inc(sem("xsq_used"), 1)

            def wait_evacuated(gn):
                l, g = divmod(gn, NG)
                name = GROUPS[g][0]
                i = int(name[-1]) if name[-1].isdigit() else 0
                if name == "latq":
                    pe.wait_ge(sem("lat_ready"), 3 * l + 2)
                elif name == "latkv":
                    pe.wait_ge(sem("lat_ready"), 3 * l + 3)
                    pe.wait_ge(sem("rope_used"), 4 * l + 1)
                elif name == "gq":
                    pe.wait_ge(sem("gqk_ready"), 6 * l + 3)
                elif name == "gk":
                    pe.wait_ge(sem("gqk_ready"), 6 * l + 6)
                elif name[:2] == "uq":
                    pe.wait_ge(sem("qn_ready"), 6 * l + 2 * i + 2)
                elif name[:2] == "kn":
                    pe.wait_ge(sem("kn_ready"), 6 * l + 3 * i + 3)
                elif name[:2] == "vm":
                    pe.wait_ge(sem("vm_ready"), 4 * l + 2 * i + 2)
                elif name[:2] == "gv":
                    pe.wait_ge(sem("gv_ready"), 4 * l + 2 * i + 2)
                elif name[:4] == "conv":
                    pe.wait_ge(sem("o_conv"), 4 * l + i + 1)
                elif name[0] == "z":
                    pe.wait_ge(sem("silu_ready"), 8 * l + 2 * i + 2)
                else:
                    pe.wait_ge(sem("x_ready"), 16 * l + 4 * i + 4)

            def weight_chunk(l, c):
                g, k = CHUNKS[c]
                name, cols, kt, nch = GROUPS[g]
                n, gn = chunk_no(l, c), l * NG + g
                s = n % SPLIT
                pe.wait_ge(sem("lo_ready"), n + 1)
                if k == 0 and gn >= 2:
                    wait_evacuated(gn - 2)
                if name[:2] in ("uq", "kn", "vm"):
                    base, mv_hi, mv_lo = 0 if name[:2] == "uq" else 3, lat_hi, lat_lo
                    pe.wait_ge(sem("latlo_ready"), 5 * (l + 1))
                else:
                    base, mv_hi, mv_lo = ROWS * k, a_hi, a_lo
                for r in range(kt):
                    if name == "latq":
                        pe.wait_ge(sem("hlo_ready"), 16 * l + base + r + 1)
                    if name == "out0":
                        pe.wait_ge(sem("ylo_ready"), 16 * l + base + r + 1)
                    hi_w = w_hi[:, s, r * cols:(r + 1) * cols]
                    lo_w = w_lo[:, s, r * cols:(r + 1) * cols]
                    first, last = k == 0 and r == 0, k == nch - 1 and r == kt - 1
                    if name[:2] in ("vm", "gv"):
                        for j in range(2):
                            ah = mv_hi[:, base + r, j * P:(j + 1) * P]
                            al = mv_lo[:, base + r, j * P:(j + 1) * P]
                            to = gbanks(gn)[j][:, 0:cols]
                            pe.matmul(to, ah, hi_w, start=first, stop=False)
                            pe.matmul(to, ah, lo_w, start=False, stop=False)
                            mm = pe.matmul(to, al, hi_w, start=False, stop=last)
                    else:
                        for j in range(cols // P):
                            to = tile_of(gn, j)
                            hi_j, lo_j = hi_w[:, j * P:(j + 1) * P], lo_w[:, j * P:(j + 1) * P]
                            ah, al = mv_hi[:, base + r, :], mv_lo[:, base + r, :]
                            pe.matmul(to, hi_j, ah, start=first and j % 2 == 0, stop=False, skip_group_check=True)
                            pe.matmul(to, hi_j, al, start=False, stop=False, skip_group_check=True)
                            mm = pe.matmul(to, lo_j, ah, start=False, stop=last, skip_group_check=True)
                mm.then_inc(sem("chunk_done"), 1)

            def kv(bk, col, d, n, hh, pr):
                r = (n % 2) * CH
                h = 2 * pr + hh
                return pe.matmul(bk[hh * DK:(hh + 1) * DK, col * P:(col + 1) * P],
                                 keT[r:r + CH, d * 2 + n // 2, hh * DK:(hh + 1) * DK],
                                 gv[r:r + CH, n // 2, h * P:(h + 1) * P], start=True, stop=True)

            def osums(n0, count, to, first, last):
                for i in range(count):
                    pe.wait_ge(sem("osq_ready"), n0 + i + 1)
                    pe.matmul(to(i), ones, sqo[:, (n0 + i) % 4, :], start=first(i), stop=last(i)
                              ).then_inc(sem("osq_used"), 1)

            pe.wait_ge(sem("const_in"), 16)
            pe.wait_ge(sem("wg_in"), 16)
            for m in range(16):
                xsum(m)
            pe.wait_ge(sem("cz_ready"), 1)
            for n in range(ADA_FIRST[0]):
                ada_chunk(n)
                if n % 4 == 3:
                    ada_turn(n // 4)
            for l in range(DEPTH):
                for c, (g, k) in enumerate(CHUNKS):
                    name = GROUPS[g][0]
                    weight_chunk(l, c)
                    if c:
                        for m in range(ada_before(l, c - 1) // 4, ada_before(l, c) // 4):
                            ada_turn(ADA_FIRST[l] // 4 + m)
                    if name == "latkv" and k == 3:
                        for i in range(5):
                            pe.wait_ge(sem("latsq_ready"), 5 * l + i + 1)
                            pe.matmul(pn[:, (i // 3) * T:(i // 3) * T + T], ones, sqx[:, i % 4, :],
                                      start=i in (0, 3), stop=i in (2, 4)).then_inc(sem("latsq_used"), 1)
                    h = c - MLA_AT - 2
                    if 0 <= h < HEADS:
                        pe.wait_ge(sem("probT_ready"), HEADS * l + h + 1)
                        if h > 0:
                            pe.wait_ge(sem("o_mla"), HEADS * l + h)
                        for kt in range(2):
                            mm = pe.matmul(pn[:, 0:T], vm[:, kt, h * P:(h + 1) * P],
                                           probT[:, kt * T:(kt + 1) * T], start=(kt == 0), stop=(kt == 1))
                        mm.then_inc(sem("pv_done"), 1)
                    h = c - MLA_AT - 1
                    if 0 <= h < HEADS:
                        pe.wait_ge(sem("probn_ready"), 2 * (HEADS * l + h) + 2)
                        if l + h > 0:
                            pe.wait_ge(sem("probT_ready"), HEADS * l + h)
                        for kt in range(2):
                            for q in range(2):
                                mm = pe.transpose(pt[:, kt * T + q * P:kt * T + (q + 1) * P],
                                                  prob[:, q, kt * P:(kt + 1) * P], ident)
                        mm.then_inc(sem("prob_used"), 1)
                    h = c - MLA_AT
                    if 0 <= h < HEADS:
                        if h == 0:
                            pe.wait_ge(sem("kr_ready"), l + 1)
                            pe.wait_ge(sem("qr_ready"), 3 * (l + 1))
                            pe.wait_ge(sem("qn_ready"), 6 * (l + 1))
                            pe.wait_ge(sem("kn_ready"), 6 * (l + 1))
                            pe.wait_ge(sem("vm_ready"), 4 * (l + 1))
                        else:
                            pe.wait_ge(sem("exp_ready"), 2 * (HEADS * l + h))
                        r = (h % 2) * DK
                        for q in range(2):
                            to = ps[:, q * T:(q + 1) * T]
                            pe.matmul(to, o[:, 6 + h, q * P:(q + 1) * P], kn[:, h, :], start=True, stop=False)
                            mm = pe.matmul(to, qr[r:r + DK, h // 2, q * P:(q + 1) * P], kr[r:r + DK, :],
                                           start=False, stop=True)
                        mm.then_inc(sem("score_ready"), 1)
                    for pr in range(PAIRS):
                        s0 = GLA_AT + GLA_STEPS * pr
                        m = PAIRS * l + pr
                        if c == s0 - 1:
                            pe.wait_ge(sem("lr_ready"), l + 1)
                            if pr == 0:
                                pe.wait_ge(sem("probT_ready"), HEADS * (l + 1))
                            else:
                                pe.wait_ge(sem("sta_ready"), 6 * m)
                            for d in range(2):
                                mm = pe.matmul(pt[:, d * T:(d + 1) * T],
                                               wgs[:, l, d * QL + pr * P:d * QL + (pr + 1) * P], lrT[:, :],
                                               start=True, stop=True)
                            mm.then_inc(sem("gate_psum"), 1)
                        if c == s0 + 1:
                            pe.wait_ge(sem("qdec_ready"), 2 * m + 2)
                            pe.wait_ge(sem("kinv_ready"), 2 * m + 2)
                            if pr == 0:
                                pe.wait_ge(sem("exp_ready"), 2 * HEADS * (l + 1))
                            else:
                                pe.wait_ge(sem("o_gla"), HEADS * l + 2 * pr)
                            for hh in range(2):
                                rows = slice(hh * DK, (hh + 1) * DK)
                                for d in range(2):
                                    for tt in range(2):
                                        tok = slice(tt * P, (tt + 1) * P)
                                        mm = pe.matmul((ps, pt)[hh][:, (d * 2 + tt) * P:(d * 2 + tt + 1) * P],
                                                       e_k[rows, d, tok], e_q[rows, d, tok], start=True, stop=True)
                                mm.then_inc(sem("gscore_ready"), 1)
                        if c == s0 + 2:
                            pe.wait_ge(sem("kend_ready"), 2 * m + 2)
                            pe.wait_ge(sem("st_ready"), 4 * m + 4)
                            for d in range(2):
                                for tt in range(2):
                                    mm = pe.transpose(pt[:, (d * 2 + tt) * P:(d * 2 + tt + 1) * P],
                                                      e_e[:, d, tt * P:(tt + 1) * P], ident)
                            mm.then_inc(sem("keT_psum"), 1)
                        if c == s0 + 3:
                            pe.wait_ge(sem("keT_ready"), m + 1)
                            pe.wait_ge(sem("gv_ready"), 4 * (l + 1))
                            for col, (d, n) in enumerate([(0, 0), (0, 2), (1, 2)]):
                                for hh in range(2):
                                    kv(ps, col, d, n, hh, pr)
                            for col, (d, n) in enumerate([(0, 1), (1, 3), (1, 1)]):
                                for hh in range(2):
                                    mm = kv(pt, col, d, n, hh, pr)
                            mm.then_inc(sem("kv_done"), 1)
                        if c == s0 + 4:
                            pe.wait_ge(sem("sta_ready"), 6 * m + 6)
                            if pr == 0:
                                pe.wait_ge(sem("root_ready"), 8 * l + 4)
                            for hh in range(2):
                                bk = (pn, ps)[hh]
                                h = 2 * pr + hh
                                rows = slice(hh * DK, (hh + 1) * DK)
                                for tt in range(2):
                                    pe.matmul(bk[:, tt * P:(tt + 1) * P], gv[:, tt, h * P:(h + 1) * P],
                                              st[:, hh, tt, :], start=(tt == 0), stop=False, skip_group_check=True)
                                for d in range(2):
                                    for i in range(3):
                                        n = i + 1 if d == 0 else 2 - i
                                        mm = pe.matmul(bk[:, n * CH:(n + 1) * CH], sta[rows, d, i, :],
                                                       e_q[rows, d, n * CH:(n + 1) * CH], start=False,
                                                       stop=(d == 1 and i == 2), skip_group_check=True)
                            mm.then_inc(sem("pair_done"), 1)
                    if c == MLAN_AT:
                        osums(16 * l, 6, lambda i: pn[:, 0:T], lambda i: i == 0, lambda i: i == 5)
                    for pr in range(PAIRS):
                        if c == GLAN_AT + pr:
                            bk = (pt, ps, pt)[pr]
                            if pr == 0:
                                pe.wait_ge(sem("sta_ready"), 6 * PAIRS * (l + 1))
                            if pr == 1:
                                pe.wait_ge(sem("o_gla"), HEADS * (l + 1))
                            if pr == 2:
                                pe.wait_ge(sem("root_ready"), 8 * l + 5)
                            osums(16 * l + 6 + 2 * pr, 2, lambda i: bk[:, i * T:(i + 1) * T],
                                  lambda i: True, lambda i: True)
                    if c == CONVN_AT:
                        pe.wait_ge(sem("o_gla"), HEADS * (l + 1))
                        osums(16 * l + 12, 4, lambda i: pn[:, 0:T], lambda i: i == 0, lambda i: i == 3)
                    if name[:3] == "out" and k == 3:
                        if name == "out0":
                            pe.wait_ge(sem("root_ready"), 8 * (l + 1))
                        for j in range(4):
                            xsum(16 * (l + 1) + 4 * int(name[3]) + j)
                    for n in range(ada_before(l, c), ada_before(l, c + 1)):
                        ada_chunk(ADA_FIRST[l] + n)

        @block.vector
        def _(dve):
            told = {}

            def tell(ins, name):
                ins.then_inc(sem(name), 1)
                told[name] = told.get(name, 0) + 1
                told["last"] = name

            def own(name):
                dve.wait_ge(sem(name), told[name])

            def settle():
                own(told["last"])

            def split_lo(n):
                l, c = divmod(n, NC)
                cols = GROUPS[CHUNKS[c][0]][1] * GROUPS[CHUNKS[c][0]][2]
                dve.wait_ge(sem("hi_ready"), n + 1)
                tell(dve.tensor_tensor(w_lo[:, n % SPLIT, 0:cols], ring[:, slot("w", n), 0:cols],
                                       w_hi[:, n % SPLIT, 0:cols], ALU.subtract), "lo_ready")

            def ada_bias(m):
                l, g, _ = ADA[4 * m]
                dve.wait_ge(sem("ada_turned"), m + 1)
                tell(dve.tensor_tensor(acol[:, l, 4 * g:4 * g + 4], pa[:, 0:4], p(l, C_ADAB + 4 * g, 4),
                                       ALU.add), "ada_biased")

            def invert(roots, cols):
                settle()
                dve.wait_ge(sem("root_ready"), roots)
                tell(dve.reciprocal(rinv[:, 0:cols], rs[:, 0:cols]), "rinv_ready")
                own("rinv_ready")

            def enter_layer(l):
                own("ada_biased")
                tell(dve.scalar_tensor_tensor(hscale[:, :], acol[:, l, 16:32], 1.0, p(l, C_NORM, 16),
                                              ALU.add, ALU.mult), "hscale_ready")
                invert(8 * l + 1, T)
                own("hscale_ready")

                def lo(t):
                    dve.wait_ge(sem("ahi_ready"), 16 * l + t + 1)
                    tell(dve.scalar_tensor_tensor(a_lo[:, t, :], tmp[:, t % 4, :], acol[:, l, t:t + 1],
                                                  a_hi[:, t, :], ALU.add, ALU.subtract), "hlo_ready")
                for t in range(KT):
                    if t >= 4:
                        lo(t - 3)
                        dve.wait_ge(sem("hlo_ready"), 16 * l + t - 3)
                    elif t == 3:
                        lo(0)
                    tell(dve.scalar_tensor_tensor(tmp[:, t % 4, :], x[:, t, :], hscale[:, t:t + 1],
                                                  rinv[:, 0:T], ALU.mult, ALU.mult), "hmul_ready")
                for t in range(KT - 3, KT):
                    lo(t)

            def rope(direct, swapped, dst, done):
                settle()
                tell(dve.tensor_tensor(ropet[:, 0, :], direct, rope_cos[:, :], ALU.mult), "rope_part")
                tell(dve.tensor_tensor(ropet[:, 1, :], swapped, rope_sin[:, :], ALU.mult), "rope_used")
                own("rope_part")
                own("rope_used")
                tell(dve.tensor_tensor(dst, ropet[:, 0, :], ropet[:, 1, :], ALU.add), done)

            dve.wait_ge(sem("const_in"), 16)
            dve.wait_ge(sem("pos_in"), 16)

            def chain(ins):
                tell(ins, "setup")
                own("setup")

            chain(dve.tensor_copy(ang[:, 0:T], pos_i[:, :]))
            chain(dve.tensor_scalar(ang[:, 0:T], ang[:, 0:T], kst[:, K_FREQ:K_FREQ + 1], None, ALU.mult))
            chain(dve.tensor_copy(ang[:, T:2 * T], ang[:, 0:T]))
            chain(dve.tensor_scalar(turns[:, 0:T], ang[:, 0:T], 0.15915494309189535, 0.25, ALU.mult, ALU.add))
            chain(dve.tensor_scalar(turns[:, T:2 * T], ang[:, 0:T], 0.15915494309189535, None, ALU.mult))
            chain(dve.tensor_scalar(turns[:, :], turns[:, :], MAGIC, None, ALU.add))
            chain(dve.tensor_scalar(turns[:, :], turns[:, :], MAGIC, None, ALU.subtract))
            for part in TWO_PI:
                chain(dve.scalar_tensor_tensor(ang[:, :], turns[:, :], -part, ang[:, :], ALU.mult, ALU.add))
            chain(dve.tensor_scalar(ang[:, 0:T], ang[:, 0:T], 1.5707963267948966, None, ALU.add))
            tell(dve.tensor_scalar(ang[:, 0:T], ang[:, 0:T], 3.1415925, -3.1415925, ALU.min, ALU.max),
                 "angle_ready")
            tell(dve.tensor_scalar(ang[:, T:2 * T], ang[:, T:2 * T], 3.1415925, -3.1415925, ALU.min, ALU.max),
                 "angle_ready")
            dve.wait_ge(sem("trig"), 2)
            chain(dve.tensor_scalar(rope_sin[:, :], rope_sin[:, :], kst[:, K_SIGN:K_SIGN + 1], None, ALU.mult))
            dve.wait_ge(sem("par_in"), 16)
            dve.wait_ge(sem("x_in"), 16)
            dve.wait_ge(sem("fin_in"), 16)
            dve.wait_ge(sem("u_zero"), 1)
            dve.wait_ge(sem("st_zero"), 1)
            for m in range(8):
                ada_bias(m)
            split_lo(0)

            for l in range(DEPTH):
                enter_layer(l)
                for c, (g, k) in enumerate(CHUNKS):
                    n = chunk_no(l, c)
                    if n + 1 < DEPTH * NC:
                        split_lo(n + 1)
                    if c:
                        for m in range(ada_before(l, c - 1) // 4, ada_before(l, c) // 4):
                            ada_bias(ADA_FIRST[l] // 4 + m)
                    name = GROUPS[g][0]
                    gn = l * NG + g
                    if k == GROUPS[g][3] - 1:
                        if name == "latkv":
                            dve.wait_ge(sem("chunk_done"), n + 1)
                            rope(tile_of(gn, 2), tile_of(gn, 3), kr[:, :], "kr_ready")
                            invert(8 * l + 3, 2 * T)
                            for i in range(5):
                                half = (i // 3) * T
                                gain = p(l, C_QG + i) if i < 3 else p(l, C_KVG + i - 3)
                                tell(dve.scalar_tensor_tensor(lat[:, i, :], lat[:, i, :], gain,
                                                              rinv[:, half:half + T], ALU.mult, ALU.mult),
                                     "latn_ready")
                            for i in range(5):
                                dve.wait_ge(sem("lathi_ready"), 5 * l + i + 1)
                                tell(dve.tensor_tensor(lat_lo[:, i, :], lat[:, i, :], lat_hi[:, i, :],
                                                       ALU.subtract), "latlo_ready")
                        elif name[:2] == "uq":
                            dve.wait_ge(sem("chunk_done"), n + 1)
                            rope(tile_of(gn, 1), tile_of(gn, 2), qr[:, int(name[2]), :], "qr_ready")
                        elif name[:4] == "conv":
                            i = int(name[4])
                            settle()
                            dve.wait_ge(sem("cc_ready"), 4 * l + i + 1)
                            tell(dve.tensor_tensor(u[:, 1:T + 1], tile_of(gn, 1), ccs[:, :], ALU.mult), "u_ready")
                            own("u_ready")
                            tell(dve.tensor_scalar(cv[:, 0, :], u[:, 0:T], p(l, C_CW + i), None, ALU.mult), "tap")
                            own("tap")
                            tell(dve.scalar_tensor_tensor(cv[:, 1, :], u[:, 1:T + 1], p(l, C_CW + 4 + i),
                                                          cv[:, 0, :], ALU.mult, ALU.add), "tap")
                            own("tap")
                            tell(dve.scalar_tensor_tensor(cv[:, 0, :], u[:, 2:T + 2], p(l, C_CW + 8 + i),
                                                          cv[:, 1, :], ALU.mult, ALU.add), "tap")
                            own("tap")
                            tell(dve.tensor_tensor(o[:, 12 + i, :], tile_of(gn, 2), cv[:, 0, :], ALU.mult),
                                 "o_conv")
                        elif name[:3] == "out":
                            i = int(name[3])
                            settle()
                            dve.wait_ge(sem("chunk_done"), n + 1)
                            for j in range(4):
                                t = 4 * i + j
                                tell(dve.scalar_tensor_tensor(x[:, t, :], tile_of(gn, j), acol[:, l, 32 + t:33 + t],
                                                              x[:, t, :], ALU.mult, ALU.add), "x_ready")
                    h = c - MLA_AT
                    if 0 <= h < HEADS:
                        settle()
                        dve.wait_ge(sem("score_ready"), HEADS * l + h + 1)
                        tell(dve.tensor_reduce(mx[:, :], ps[:, :].rearrange("p (a b) -> p a b", a=2), AX.X,
                                               ALU.max), "mx_ready")
                        own("mx_ready")
                        tell(dve.tensor_scalar(nmx[:, :], mx[:, :], -SM_SCALE, None, ALU.mult), "nmx_ready")
                        dve.wait_ge(sem("exp_ready"), 2 * (HEADS * l + h) + 2)
                        tell(dve.reciprocal(rsi[:, :], rsum[:, :]), "rsi_ready")
                        own("rsi_ready")
                        for q in range(2):
                            tell(dve.tensor_scalar(prob[:, q, :], prob[:, q, :], rsi[:, q:q + 1], None, ALU.mult),
                                 "probn_ready")
                    for pr in range(PAIRS):
                        s0 = GLA_AT + GLA_STEPS * pr
                        m = PAIRS * l + pr
                        if c == s0:
                            settle()
                            dve.wait_ge(sem("gate_psum"), m + 1)
                            for d in range(2):
                                tell(dve.tensor_scalar(gx[:, d * T:(d + 1) * T], pt[:, d * T:(d + 1) * T],
                                                       p(l, (C_BGF, C_BGB)[d] + pr), None, ALU.add), "gx_ready")
                            own("gx_ready")
                            dve.wait_ge(sem("ln_ready"), m + 1)
                            tell(dve.scalar_tensor_tensor(gx[:, :], gx[:, :], 0.0, gt[:, :], ALU.min,
                                                          ALU.subtract), "la_ready")
                            own("la_ready")
                            scan = kst[:, K_SCAN:K_SCAN + T]
                            tell(dve.tensor_tensor_scan(cs[:, 0:T], scan, gx[:, 0:T], 0.0, ALU.mult, ALU.add),
                                 "cs_ready")
                            tell(dve.tensor_tensor_scan(cs[:, 2 * T - 1:T - 1:-1], scan, gx[:, 2 * T - 1:T - 1:-1],
                                                        0.0, ALU.mult, ALU.add), "cs_ready")
                            own("cs_ready")
                            if m:
                                dve.wait_ge(sem("keT_psum"), m)
                            for d in range(2):
                                b = cs[:, d * T:(d + 1) * T].rearrange("p (n s) -> p n s", n=NCH)
                                end = b[:, :, CH - 1:CH] if d == 0 else b[:, :, 0:1]
                                tell(dve.tensor_tensor(e_e[:, d, :].rearrange("p (n s) -> p n s", n=NCH),
                                                       end.to_broadcast([P, NCH, CH]), b, ALU.subtract),
                                     "bdiff_ready")
                            dve.wait_ge(sem("expb_ready"), 2 * m + 2)
                            for d in range(2):
                                b = e_q[:, d, :].rearrange("p (n s) -> p n s", n=NCH)
                                end = b[:, :, CH - 1] if d == 0 else b[:, :, 0]
                                tell(dve.tensor_copy(dec[:, d, :], end), "dec_ready")
                            own("dec_ready")
                            for d in range(2):
                                tell(dve.scalar_tensor_tensor(e_q[:, d, :], o[:, 2 * pr, :], DK ** -0.5,
                                                              e_q[:, d, :], ALU.mult, ALU.mult), "qdec_ready")
                            for d in range(2):
                                tell(dve.tensor_tensor(e_k[:, d, :], o[:, 2 * pr + 1, :], e_k[:, d, :], ALU.mult),
                                     "kinv_ready")
                            dve.wait_ge(sem("expe_ready"), m + 1)
                            for d in range(2):
                                tell(dve.tensor_tensor(e_e[:, d, :], o[:, 2 * pr + 1, :], e_e[:, d, :], ALU.mult),
                                     "kend_ready")
                        if c == s0 + 1:
                            settle()
                            if m:
                                dve.wait_ge(sem("pair_done"), m)
                            for d, mask in enumerate((K_MF, K_MB)):
                                if d:
                                    settle()
                                for hh in range(2):
                                    dve.wait_ge(sem("gscore_ready"), 2 * m + hh + 1)
                                    tell(dve.copy_predicated(
                                        st[:, hh, :, :].rearrange("p a b -> p (a b)"),
                                        kst[:, mask:mask + T].bitcast(I32),
                                        (ps, pt)[hh][:, d * T:(d + 1) * T]), "st_ready")
                        if c == s0 + 3:
                            settle()
                            dve.wait_ge(sem("kv_done"), m + 1)
                            even = lambda i: ps[:, i * P:(i + 1) * P]
                            odd = lambda i: pt[:, i * P:(i + 1) * P]
                            tell(dve.tensor_copy(sta[:, 0, 0, :], even(0)), "sta_ready")
                            tell(dve.tensor_copy(sta[:, 1, 0, :], odd(1)), "sta_ready")
                            own("sta_ready")
                            tell(dve.scalar_tensor_tensor(sta[:, 0, 1, :], sta[:, 0, 0, :], dec[:, 0, 1:2],
                                                          odd(0), ALU.mult, ALU.add), "sta_ready")
                            tell(dve.scalar_tensor_tensor(sta[:, 1, 1, :], sta[:, 1, 0, :], dec[:, 1, 2:3],
                                                          even(2), ALU.mult, ALU.add), "sta_ready")
                            own("sta_ready")
                            tell(dve.scalar_tensor_tensor(sta[:, 0, 2, :], sta[:, 0, 1, :], dec[:, 0, 2:3],
                                                          even(1), ALU.mult, ALU.add), "sta_ready")
                            tell(dve.scalar_tensor_tensor(sta[:, 1, 2, :], sta[:, 1, 1, :], dec[:, 1, 1:2],
                                                          odd(2), ALU.mult, ALU.add), "sta_ready")
                    if c == MLAN_AT:
                        invert(8 * l + 4, T)
                        for i in range(6):
                            tell(dve.scalar_tensor_tensor(o[:, 6 + i, :], o[:, 6 + i, :], p(l, C_MLAG + i),
                                                          rinv[:, 0:T], ALU.mult, ALU.mult), "onorm_mla")
                    for pr in range(PAIRS):
                        if c == GLAN_AT + pr:
                            invert(8 * l + 5 + pr, 2 * T)
                            two = o[:, 2 * pr:2 * pr + 2, :].rearrange("p a b -> p (a b)")
                            tell(dve.scalar_tensor_tensor(two, two, p(l, C_GLAG), rinv[:, :], ALU.mult, ALU.mult),
                                 "onorm_gla")
                    if c == CONVN_AT:
                        invert(8 * l + 8, T)
                        for i in range(4):
                            tell(dve.scalar_tensor_tensor(o[:, 12 + i, :], o[:, 12 + i, :], p(l, C_CG + i),
                                                          rinv[:, 0:T], ALU.mult, ALU.mult), "onorm_conv")
                    if c == LAST_CHUNK["z3"]:
                        settle()
                        for t in range(KT):
                            dve.wait_ge(sem("yhi_ready"), 16 * l + t + 1)
                            tell(dve.tensor_tensor(a_lo[:, t, :], o[:, Y_ORDER[t], :], a_hi[:, t, :],
                                                   ALU.subtract), "ylo_ready")
            invert(8 * DEPTH + 1, T)
            for t in range(KT):
                tell(dve.scalar_tensor_tensor(o[:, t, :], x[:, t, :], fing[:, t:t + 1], rinv[:, 0:T],
                                              ALU.mult, ALU.mult), "final_ready")


def pack_stream(w_in, w_out, w_uq, w_ukv):
    import numpy as np
    at = np.cumsum([0, 384, 384, 768, 32, 384, 256, 64, 512, 512, 512, 2048])
    gq, gk, gv, lr, mq, mkv, mkr, cb, cc, cx, z = (np.arange(a, b) for a, b in zip(at[:-1], at[1:]))
    none = -np.ones(P, int)
    lr_tile = none.copy()
    lr_tile[0:16], lr_tile[32:48] = lr[0:16], lr[16:32]
    swap = lambda a: np.concatenate([a[32:], a[:32]])
    head = lambda h, w: np.arange(w * h, w * (h + 1))
    cols = {"latq": np.concatenate([lr_tile, mq]),
            "latkv": np.concatenate([mkv, mkr, mkr, swap(mkr), swap(mkr)]), "gq": gq, "gk": gk}
    for i in range(3):
        a, b = head(2 * i, 192), head(2 * i + 1, 192)
        cols[f"uq{i}"] = np.concatenate([a[:128], a[128:], b[128:], swap(a[128:]), swap(b[128:]), b[:128]])
    for i in range(2):
        cols[f"kn{i}"] = np.concatenate([head(h, 256)[:128] for h in range(3 * i, 3 * i + 3)])
        cols[f"vm{i}"] = np.concatenate([head(h, 256)[128:] for h in range(3 * i, 3 * i + 3)])
        cols[f"gv{i}"] = gv[384 * i:384 * i + 384]
    for i in range(CONVT):
        s = slice(P * i, P * i + P)
        cols[f"conv{i}"] = np.concatenate([cc[s], cx[s], cb[s]])
    for i in range(4):
        cols[f"z{i}"] = np.concatenate([z[P * t:P * t + P] for t in Y_ORDER[4 * i:4 * i + 4]])
        cols[f"out{i}"] = np.arange(512 * i, 512 * i + 512)
    y_rows = np.concatenate([np.arange(P * t, P * t + P) for t in Y_ORDER])
    out = np.zeros((DEPTH, STREAM_AT[-1]), w_in.dtype)
    for l in range(DEPTH):
        for c, (g, k) in enumerate(CHUNKS):
            name, width, kt, _ = GROUPS[g]
            src = w_uq[l] if name[:2] == "uq" else w_ukv[l] if name[:2] in ("kn", "vm") else \
                w_out[l][y_rows] if name[:3] == "out" else w_in[l]
            rows = src[k * kt * P:(k + 1) * kt * P]
            part = np.where(cols[name] >= 0, rows[:, np.maximum(cols[name], 0)], np.zeros((), w_in.dtype))
            out[l, STREAM_AT[c]:STREAM_AT[c + 1]] = part.reshape(kt, P, width).transpose(1, 0, 2).ravel()
    return out


def kernel(**inputs):
    import numpy as np
    import concourse.bacc as _bacc
    from concourse import mybir as _mybir
    from concourse.bass_utils import run_bass_kernel_spmd as _run

    a = {k: np.asarray(v) for k, v in inputs.items()}
    f4 = np.float32

    def tiles(v):
        return np.swapaxes(v.reshape(*v.shape[:-1], -1, P), -1, -2)

    par = np.zeros((P, DEPTH, SMALL), f4)
    put = lambda col, v: par.__setitem__((slice(None), slice(None), slice(col, col + v.shape[-1])),
                                         np.moveaxis(v, 0, 1))
    put(C_NORM, tiles(a["norm_g"]))
    put(C_ADAB, tiles(a["ada_b"]))
    put(C_BGF, tiles(a["gla_bg_f"]))
    put(C_BGB, tiles(a["gla_bg_b"]))
    put(C_GLAG, tiles(a["gla_norm_g"]))
    put(C_QG, tiles(a["mla_q_norm_g"]))
    put(C_KVG, tiles(a["mla_kv_norm_g"]))
    put(C_MLAG, tiles(a["mla_out_g"]))
    for tap in range(3):
        put(C_CW + 4 * tap, tiles(a["conv_w"][:, tap]))
    put(C_CG, tiles(a["conv_out_g"]))
    wg = np.zeros((64, DEPTH, 2 * QL), f4)
    wg[0:RANK, :, 0:QL] = a["gla_wg_f"].transpose(1, 0, 2)
    wg[32:32 + RANK, :, QL:] = a["gla_wg_b"].transpose(1, 0, 2)

    const = np.zeros((P, CONST), f4)
    const[:, K_ONES:K_ONES + P] = 1
    const[:, K_ID:K_ID + P] = np.eye(P)
    j, i = np.arange(P)[:, None], np.arange(T)[None, :] % P
    same = j // CH == i // CH
    const[:, K_MF:K_MF + T] = same & (j <= i)
    const[:, K_MB:K_MB + T] = same & (j > i)
    const[:, K_SCAN:K_SCAN + T] = np.arange(T) % CH != 0
    const[:, K_SEL] = np.arange(P) % 32 == 0
    const[:, K_SIGN] = np.where(np.arange(P) % 64 < 32, -1, 1)
    const[:, K_FREQ] = np.float32(10000.0) ** (-(np.arange(P) % 32).astype(f4) * 2 / np.float32(64))
    const[:, K_EPS] = EPS

    ada = a["ada_w"].reshape(DEPTH, 4, ROWS, P, ADA_GROUPS, WIDE).transpose(0, 4, 1, 3, 2, 5)
    arrays = {
        "xT": np.ascontiguousarray(a["x"][0].T.reshape(KT, P, T).transpose(1, 0, 2)),
        "cT": np.ascontiguousarray(tiles(a["c"][0])),
        "posr": np.ascontiguousarray(a["positions"]),
        "wstream": pack_stream(a["w_in"], a["w_out"], a["mla_w_uq"], a["mla_w_ukv"]),
        "adastream": np.ascontiguousarray(ada).reshape(DEPTH, ADA_GROUPS, 4, P, ROWS * WIDE),
        "wg": wg, "small": par, "finalg": np.ascontiguousarray(tiles(a["final_g"])), "const": const,
    }
    nc = _bacc.Bacc("TRN2", target_bir_lowering=False, num_devices=1,
                     dynamic_dma_scratch_size=1024)
    aps = {n: nc.dram_tensor(n, v.shape, _mybir.dt.from_np(v.dtype), kind="ExternalInput").ap()
           for n, v in arrays.items()}
    out = nc.dram_tensor("out", (P, KT, T), _mybir.dt.float32, kind="ExternalOutput").ap()
    build(nc, out=out, **aps)
    r = _run(nc, [arrays], core_ids=[0]).results[0]["out"]
    return np.ascontiguousarray(r.transpose(1, 0, 2).reshape(D, T).T)[None]
```

```python
from contextlib import ExitStack

import concourse.bass as bass
from concourse import mybir

P = 128
D = 2048
T = 256
DEPTH = 2
KT = D // P
HEADS = 6
PAIRS = HEADS // 2
DK = 64
CH = 64
NCH = T // CH
RANK = 16
QL, KVL = 384, 256
CONVT = 4
EPS = 1e-6
ROWS = 4
RING, SPLIT = 5, 2
WIDE = 512
ADA_GROUPS = 3 * D // WIDE
SM_SCALE = (128 + 64) ** -0.5

GROUPS = (
    [("latq", 512, ROWS, 4), ("latkv", 256, ROWS, 4), ("gq", 384, ROWS, 4), ("gk", 384, ROWS, 4)]
    + [(f"gv{i}", 384, ROWS, 4) for i in range(2)]
    + [(f"conv{i}", 384, ROWS, 4) for i in range(CONVT)]
    + [(f"uq{i}", 384, 3, 1) for i in range(3)]
    + [(f"kn{i}", 384, 2, 1) for i in range(2)]
    + [(f"vm{i}", 384, 2, 1) for i in range(2)]
    + [(f"z{i}", 512, ROWS, 4) for i in range(4)]
    + [(f"out{i}", 512, ROWS, 4) for i in range(4)]
)
GROUP_AT = {g[0]: n for n, g in enumerate(GROUPS)}
NG = len(GROUPS)
SIDE = 4
CHUNKS = [(n, k) for k in range(4) for n in range(SIDE)] + [
    (n, k) for n, g in enumerate(GROUPS) if n >= SIDE for k in range(g[3])]
NC = len(CHUNKS)
FIRST_CHUNK = {g: min(i for i, (n, _) in enumerate(CHUNKS) if GROUPS[n][0] == g) for g in GROUP_AT}
LAST_CHUNK = {g: max(i for i, (n, _) in enumerate(CHUNKS) if GROUPS[n][0] == g) for g in GROUP_AT}
SIZES = [P * GROUPS[n][1] * GROUPS[n][2] for n, _ in CHUNKS]
STREAM_AT = [sum(SIZES[:i]) for i in range(NC + 1)]
Y_ORDER = [0, 1, 2, 3, 12, 13, 14, 15, 4, 5, 6, 7, 8, 9, 10, 11]

C_NORM, C_ADAB, C_BGF, C_BGB, C_GLAG, C_QG, C_KVG, C_MLAG, C_CW, C_CG = (
    0, 16, 64, 67, 70, 71, 74, 76, 82, 94)
SMALL = 98
K_ONES, K_ID, K_MF, K_MB, K_SCAN, K_SEL, K_SIGN, K_FREQ, K_EPS = 0, 128, 256, 512, 768, 1024, 1025, 1026, 1027
CONST = 1028

GLA_AT = LAST_CHUNK["gv0"]
GLA_STEPS = 5
GLA_OUT = 6
GLAN_AT = GLA_AT + GLA_STEPS * (PAIRS - 1) + GLA_OUT + 1
CONVN_AT = LAST_CHUNK["conv3"] + 2
MLA_AT = LAST_CHUNK["vm1"] + 2
MLAN_AT = MLA_AT + HEADS + 3
PP_GROUPS = [g[0] for g in GROUPS if g[0] not in ("gq", "gk")]
LAT_AT = SIDE * 4
MAGIC = 1.5 * 2.0 ** 23
TWO_PI = (6.28125, 2029 / 2.0 ** 20, 6.283185307179586 - 6.28125 - 2029 / 2.0 ** 20)


def ada_plan(layer):
    first = [(0, g) for j in range(4) for g in (j, 4 + j)] if layer == 0 else []
    after = [(layer + 1, g) for g in range(8)] if layer + 1 < DEPTH else []
    return first + [(layer, g) for g in range(8, 12)] + after


def ada_before(layer, c):
    total = 4 * len(ada_plan(layer))
    if layer:
        return min(total, 4 + (total - 4) * max(c, 0) // (NC - 10))
    if c <= 16:
        return min(32, 8 + 2 * c)
    return min(total, 32 + (total - 32) * (c - 16) // (NC - 26))


def h_due(l, c):
    return l == 0 and c in (3, 7, 11)


def turns_in(l, c):
    if c == 0 or h_due(l, c - 1):
        return range(0)
    return range(ada_before(l, c - 1) // 4, ada_before(l, c) // 4)


ADA_FIRST = [0]
for _l in range(DEPTH):
    ADA_FIRST.append(ADA_FIRST[-1] + 4 * len(ada_plan(_l)))
LOADS = []
for _l in range(DEPTH):
    LOADS += [("a", ADA_FIRST[_l] + n) for n in range(ada_before(_l, 0))]
    if _l == 0:
        LOADS.append(("w", 0))
    for _c in range(NC):
        LOADS += [("w", _l * NC + _c + 1)] if _l * NC + _c + 1 < DEPTH * NC else []
        if _c + 1 < NC:
            LOADS += [("a", ADA_FIRST[_l] + n) for n in range(ada_before(_l, _c), ada_before(_l, _c + 1))]
PLACE = {key: i for i, key in enumerate(LOADS)}


def build(nc, xT, cT, posr, wstream, adastream, wg, small, finalg, const, out):
    F32, F32R, I32 = mybir.dt.float32, mybir.dt.float32r, mybir.dt.int32
    ALU, ACT, AX = mybir.AluOpType, mybir.ActivationFunctionType, mybir.AxisListType
    with ExitStack() as ctx:
        def sb(name, shape, dt=F32):
            return ctx.enter_context(nc.sbuf_tensor(name, shape, dt))

        def bank(name):
            return ctx.enter_context(nc.psum_tensor(name, [P, 512], F32))

        sems = {}

        def sem(name):
            if name not in sems:
                sems[name] = ctx.enter_context(nc.semaphore(name))
            return sems[name]

        x = sb("x", [P, KT, T])
        a_hi = sb("a_hi", [P, KT, T], F32R)
        a_lo = sb("a_lo", [P, KT, T], F32R)
        o = sb("o", [P, KT, T])
        ring = sb("ring", [P, RING, ROWS * WIDE])
        w_hi = sb("w_hi", [P, SPLIT, ROWS * WIDE], F32R)
        w_lo = sb("w_lo", [P, SPLIT, ROWS * WIDE], F32R)
        arow = sb("arow", [P, WIDE])
        acol = sb("acol", [P, DEPTH, 48])
        hscale = sb("hscale", [P, KT])
        ct = sb("ct", [P, KT])
        cz = sb("cz", [P, KT, 32])
        asum = sb("asum", [P, 4])
        kst = sb("kst", [P, CONST])
        par = sb("par", [P, DEPTH, SMALL])
        fing = sb("fing", [P, KT])
        wgs = sb("wgs", [P, DEPTH, 2 * QL])
        pos_i = sb("pos_i", [P, T], I32)
        rope_cos = sb("rope_cos", [P, T])
        rope_sin = sb("rope_sin", [P, T])
        sqx = sb("sqx", [P, 4, T])
        sqo = sb("sqo", [P, 4, T])
        rs = sb("rs", [P, 2 * T])
        rinv = sb("rinv", [P, 2 * T])
        rstd = sb("rstd", [P, T])
        tmp = sb("tmp", [P, 4, T])
        gx = tmp[:, 0:2, :].rearrange("p a b -> p (a b)")
        gt = tmp[:, 2:4, :].rearrange("p a b -> p (a b)")
        sz = tmp[:, :, :].rearrange("p (j a) b -> p j (a b)", j=2)
        lat = sb("lat", [P, HEADS, T])
        kn = lat
        lat_hi = sb("lat_hi", [P, 5, T], F32R)
        lat_lo = sb("lat_lo", [P, 5, T], F32R)
        kr = sb("kr", [P, T])
        qr = sb("qr", [P, PAIRS, T])
        cv = sb("cv", [P, 2, T])
        ropet = cv
        mx = sb("mx", [P, 2])
        nmx = sb("nmx", [P, 2])
        rsum = sb("rsum", [P, 2])
        rsi = sb("rsi", [P, 2])
        lrT = sb("lrT", [P, T])
        e_q = sb("e_q", [P, 2, T])
        e_k = sb("e_k", [P, 2, T])
        prob, probT = e_q, e_k[:, :, :].rearrange("p a b -> p (a b)")
        vm = sb("vm", [P, 2, HEADS * P])
        gla = vm[:, :, :].rearrange("p a b -> p (a b)")
        cs = gla[:, 0:2 * T]
        e_e = gla[:, 2 * T:4 * T].rearrange("p (a b) -> p a b", a=2)
        keT = gla[:, 4 * T:6 * T].rearrange("p (a b) -> p a b", a=4)
        ang, turns = cs, gx
        dec = sb("dec", [P, 2, NCH])
        gv = sb("gv", [P, 2, HEADS * P])
        st = sb("st", [P, 2, 2, P])
        sta = sb("sta", [P, 2, 3, P])
        ccs = sb("ccs", [P, T])
        u = sb("u", [P, T + 2])

        pp = [bank(f"pp{i}") for i in range(4)]
        pa, ps, pt, pn = bank("pa"), bank("ps"), bank("pt"), bank("pn")

        ones, ident = kst[:, K_ONES:K_ONES + P], kst[:, K_ID:K_ID + P]
        eps = kst[:, K_EPS:K_EPS + 1]

        def chunk_no(l, c):
            return l * NC + c

        def tile_of(l, name, j):
            if name in ("gq", "gk"):
                half = j + 3 * (name == "gk")
                return (ps, pt, pn)[half // 2][:, (half % 2) * T:(half % 2) * T + T]
            return gbanks(l, name)[j // 2][:, (j % 2) * T:(j % 2) * T + T]

        def opens_bank(name, j):
            return (j + 3 * (name == "gk")) % 2 == 0

        def pp_no(l, name):
            return l * len(PP_GROUPS) + PP_GROUPS.index(name)

        def gbanks(l, name):
            n = pp_no(l, name)
            return pp[2 * (n % 2)], pp[2 * (n % 2) + 1]

        def p(l, col, n=1):
            return par[:, l, col:col + n]

        ADA = [(l, g, k) for q in range(DEPTH) for l, g in ada_plan(q) for k in range(4)]

        def slot(kind, n):
            return PLACE[kind, n] % RING

        def landed(eng, kind, n):
            i = PLACE[kind, n]
            eng.wait_ge(sem(f"ring_in{i % RING}"), 16 * (i // RING + 1))

        block = ctx.enter_context(nc.Block())

        @block.sync
        def _(sp):
            sp.dma_start(ct[:, :], cT).then_inc(sem("c_in"), 16)
            sp.dma_start(kst[:, :], const).then_inc(sem("const_in"), 16)
            sp.dma_start(pos_i[:, :], posr.partition_broadcast(P)).then_inc(sem("pos_in"), 16)
            sp.dma_start(par[:, :, :], small).then_inc(sem("par_in"), 16)
            for i, (kind, n) in enumerate(LOADS):
                if i >= RING:
                    before, m = LOADS[i - RING]
                    if before == "a":
                        sp.wait_ge(sem("ada_used"), m + 1)
                    else:
                        sp.wait_ge(sem("lo_ready"), m + 1)
                if kind == "a":
                    l, g, k = ADA[n]
                    src, cols = adastream[l, g, k], ROWS * WIDE
                else:
                    l, c = divmod(n, NC)
                    cols = GROUPS[CHUNKS[c][0]][1] * GROUPS[CHUNKS[c][0]][2]
                    src = wstream[l, STREAM_AT[c]:STREAM_AT[c + 1]].rearrange("(p n) -> p n", p=P)
                sp.dma_start(ring[:, i % RING, 0:cols], src).then_inc(sem(f"ring_in{i % RING}"), 16)
                if i == RING - 1:
                    sp.dma_start(x[:, :, :], xT).then_inc(sem("x_in"), 16)
                    sp.dma_start(wgs[DK:P, :, :], wg).then_inc(sem("wg_in"), 16)
                    sp.dma_start(fing[:, :], finalg).then_inc(sem("fin_in"), 16)
            for t in range(KT):
                sp.wait_ge(sem("final_ready"), t + 1)
                sp.dma_start(out[:, t, :], o[:, t, :]).then_inc(sem("out_done"), 16)
            sp.wait_ge(sem("out_done"), 16 * KT)

        @block.gpsimd
        def _(pool):
            pool.memset(cz[:, :, :], 0.0).then_inc(sem("cz_zero"), 1)
            pool.memset(st[:, :, :, :], 0.0).then_inc(sem("st_zero"), 1)
            pool.memset(u[:, :], 0.0).then_inc(sem("u_zero"), 1)

            def squares(tiles, ready, first):
                for i, t in enumerate(tiles):
                    n = first + i
                    if n >= 4:
                        pool.wait_ge(sem("osq_used"), n - 3)
                    pool.wait_ge(*ready(i))
                    pool.tensor_tensor(sqo[:, n % 4, :], o[:, t, :], o[:, t, :], ALU.mult
                                       ).then_inc(sem("osq_ready"), 1)

            def gate_z(l, i):
                for j in range(2):
                    pool.wait_ge(sem("silu_ready"), 8 * l + 2 * i + j + 1)
                    t = Y_ORDER[4 * i + 2 * j]
                    if i == 0:
                        pool.wait_ge(sem("onorm_gla"), 3 * (l + 1))
                    elif i == 1:
                        pool.wait_ge(sem("onorm_conv"), 4 * (l + 1))
                    else:
                        pool.wait_ge(sem("onorm_mla"), 6 * (l + 1))
                    pool.tensor_tensor(o[:, t:t + 2, :], o[:, t:t + 2, :],
                                       sz[:, j, :].rearrange("p (a b) -> p a b", a=2), ALU.mult
                                       ).then_inc(sem("y_ready"), 1)

            for l in range(DEPTH):
                for pr in range(PAIRS):
                    m = PAIRS * l + pr
                    key = o[:, 2 * pr + 1:2 * pr + 2, :].to_broadcast([P, 2, T])
                    pool.wait_ge(sem("expb_ready"), 2 * m + 2)
                    pool.tensor_tensor(e_k[:, :, :], key, e_k[:, :, :], ALU.mult).then_inc(sem("kinv_ready"), 1)
                    pool.wait_ge(sem("expe_ready"), m + 1)
                    pool.tensor_tensor(e_e[:, :, :], key, e_e[:, :, :], ALU.mult).then_inc(sem("kend_ready"), 1)
                squares(range(0, 6), lambda i: (sem("o_gla"), 6 * l + i + 1), 16 * l)
                squares(range(12, 16), lambda i: (sem("o_conv"), 4 * l + i + 1), 16 * l + 6)
                gate_z(l, 0)
                squares(range(6, 12), lambda i: (sem("o_mla"), 6 * l + i + 1), 16 * l + 10)
                for i in range(1, 4):
                    gate_z(l, i)

        @block.scalar
        def _(act):
            A = act.activation

            def split_hi(n):
                g, _ = CHUNKS[n % NC]
                cols = GROUPS[g][1] * GROUPS[g][2]
                landed(act, "w", n)
                if n >= SPLIT:
                    act.wait_ge(sem("chunk_done"), n - SPLIT + 1)
                A(w_hi[:, n % SPLIT, 0:cols], ring[:, slot("w", n), 0:cols], ACT.Identity
                  ).then_inc(sem("hi_ready"), 1)

            def ada_rows(m):
                act.wait_ge(sem("ada_used"), 4 * m + 4)
                if m >= 1:
                    act.wait_ge(sem("ada_turned"), m)
                A(arow[:, :], pa[:, :], ACT.Identity).then_inc(sem("arow_ready"), 1)

            def root(psum, lo, hi, width, norms_before):
                if norms_before:
                    act.wait_ge(sem("rinv_ready"), norms_before)
                A(rs[:, lo:hi], psum, ACT.Sqrt, bias=eps, scale=1.0 / width).then_inc(sem("root_ready"), 1)

            def h_hi(l, t):
                act.wait_ge(sem("hmul_ready"), 16 * l + t + 1)
                if t == 0 and l > 0:
                    act.wait_ge(sem("chunk_done"), chunk_no(l, 0))
                if t % 4 == 0:
                    act.wait_ge(sem("shift_ready"), 4 * l + t // 4 + 1)
                A(a_hi[:, t, :], tmp[:, t % 4, :], ACT.Identity, bias=acol[:, l, t:t + 1]
                  ).then_inc(sem("ahi_ready"), 1)

            def square_x(m):
                if m >= 16:
                    act.wait_ge(sem("x_ready"), m - 15)
                if m >= 4:
                    act.wait_ge(sem("xsq_used"), m - 3)
                A(sqx[:, m % 4, :], x[:, m % 16, :], ACT.Square).then_inc(sem("xsq_ready"), 1)

            def y_hi(l, part):
                act.wait_ge(sem("chunk_done"), chunk_no(l, FIRST_CHUNK["z3"] + part) + 1)
                for t in (4 * part, 4 * part + 2):
                    act.wait_ge(sem("y_ready"), 8 * l + t // 2 + 1)
                    copy(a_hi[:, t:t + 2, :], o[:, Y_ORDER[t]:Y_ORDER[t] + 2, :], "yhi_ready")

            def copy(dst, src, done):
                A(dst, src, ACT.Identity).then_inc(sem(done), 1)

            act.wait_ge(sem("c_in"), 16)
            act.wait_ge(sem("cz_zero"), 1)
            A(cz[:, :, 0], ct[:, :], ACT.Silu).then_inc(sem("cz_ready"), 1)
            ada_rows(0)
            act.wait_ge(sem("angle_ready"), 2)
            A(rope_cos[:, :], ang[:, 0:T], ACT.Sin).then_inc(sem("trig"), 1)
            A(rope_sin[:, :], ang[:, T:2 * T], ACT.Sin).then_inc(sem("trig"), 1)
            act.wait_ge(sem("x_in"), 16)
            act.wait_ge(sem("const_in"), 16)
            for m in range(16):
                square_x(m)
            act.wait_ge(sem("xsq_used"), 16)
            root(ps[:, 0:T], 0, T, D, 0)
            split_hi(0)

            for l in range(DEPTH):
                for m in range(1 if l == 0 else 0, ada_before(l, 0) // 4):
                    ada_rows(ADA_FIRST[l] // 4 + m)
                for t in range(4):
                    h_hi(l, t)
                for c, (g, k) in enumerate(CHUNKS):
                    n = chunk_no(l, c)
                    if n + 1 < DEPTH * NC:
                        split_hi(n + 1)
                    if l > 0 and c % 4 == 2 and c < 12:
                        for t in range(c + 2, c + 6):
                            h_hi(l, t)
                    name = GROUPS[g][0]
                    gn = l * NG + g
                    i = int(name[-1]) if name[-1].isdigit() else 0
                    if k == GROUPS[g][3] - 1:
                        act.wait_ge(sem("chunk_done"), n + 1)
                        if name == "latq":
                            b0, b1 = gbanks(l, name)
                            act.wait_ge(sem("rope_used"), 4 * l + 1)
                            copy(lrT[DK:P, :], b0[DK:P, 0:T], "lr_ready")
                            copy(lat[:, 0, :], b0[:, T:2 * T], "lat_ready")
                            copy(lat[:, 1:3, :], b1[:, :].rearrange("p (a b) -> p a b", a=2), "lat_ready")
                        elif name == "latkv":
                            copy(lat[:, 3:5, :], gbanks(l, name)[0][:, :].rearrange("p (a b) -> p a b", a=2),
                                 "lat_ready")
                        elif name == "gk":
                            for i in range(6):
                                copy(o[:, 2 * (i % 3) + i // 3, :], tile_of(l, ("gq", "gk")[i // 3], i % 3),
                                     "gqk_ready")
                        elif name[:2] == "uq":
                            act.wait_ge(sem("rope_used"), 4 * l + i + 2)
                            copy(o[:, 6 + 2 * i, :], tile_of(l, name, 0), "qn_ready")
                            copy(o[:, 7 + 2 * i, :], tile_of(l, name, 2), "qn_ready")
                        elif name[:2] == "kn":
                            for j in range(3):
                                copy(kn[:, 3 * i + j, :], tile_of(l, name, j), "kn_ready")
                        elif name[:2] in ("vm", "gv"):
                            dst, done = (vm, "vm_ready") if name[:2] == "vm" else (gv, "gv_ready")
                            for j in range(2):
                                copy(dst[:, j, 384 * i:384 * i + 384], gbanks(l, name)[j][:, 0:384], done)
                        elif name[:4] == "conv":
                            if i + l > 0:
                                act.wait_ge(sem("u_ready"), 4 * l + i)
                            copy(ccs[:, :], tile_of(l, name, 0), "cc_ready")
                        elif name[0] == "z":
                            for j in range(2):
                                m = 8 * l + 2 * i + j
                                if m >= 2:
                                    act.wait_ge(sem("y_ready"), m - 1)
                                A(sz[:, j, :], gbanks(l, name)[j][:, :], ACT.Silu).then_inc(sem("silu_ready"), 1)
                    if c == LAT_AT:
                        act.wait_ge(sem("lat_ready"), 3 * (l + 1))
                        for i in range(5):
                            if i == 4:
                                act.wait_ge(sem("latsq_used"), 5 * l + 1)
                            A(sqx[:, i % 4, :], lat[:, i, :], ACT.Square).then_inc(sem("latsq_ready"), 1)
                        act.wait_ge(sem("latsq_used"), 5 * l + 5)
                        root(pn[:, 0:T], 0, T, QL, 7 * l + 1)
                        root(pn[:, T:2 * T], T, 2 * T, KVL, 7 * l + 1)
                    if c == LAT_AT + 1:
                        for i in range(5):
                            act.wait_ge(sem("latn_ready"), 5 * l + i + 1)
                            copy(lat_hi[:, i, :], lat[:, i, :], "lathi_ready")
                    h = c - MLA_AT - 2
                    if 0 <= h < HEADS:
                        act.wait_ge(sem("pv_done"), HEADS * l + h + 1)
                        copy(o[:, 6 + h, :], pn[:, 0:T], "o_mla")
                    h = c - MLA_AT - 1
                    if 0 <= h < HEADS:
                        act.wait_ge(sem("prob_used"), HEADS * l + h + 1)
                        if l + h > 0:
                            act.wait_ge(sem("pv_done"), HEADS * l + h)
                        copy(probT[:, :], pt[:, :], "probT_ready")
                    h = c - MLA_AT
                    if 0 <= h < HEADS:
                        act.wait_ge(sem("nmx_ready"), HEADS * l + h + 1)
                        if l + h > 0:
                            act.wait_ge(sem("prob_used"), HEADS * l + h)
                        for q in range(2):
                            A(prob[:, q, :], ps[:, q * T:q * T + T], ACT.Exp, bias=nmx[:, q:q + 1],
                              scale=SM_SCALE, accum_out=rsum[:, q:q + 1]).then_inc(sem("exp_ready"), 1)
                    for pr in range(PAIRS):
                        s0 = GLA_AT + GLA_STEPS * pr
                        m = PAIRS * l + pr
                        if c == s0:
                            act.wait_ge(sem("gx_ready"), 2 * m + 2)
                            A(gt[:, :], gx[:, :], ACT.Abs).then_inc(sem("abs_ready"), 1)
                            act.wait_ge(sem("abs_ready"), m + 1)
                            A(gt[:, :], gt[:, :], ACT.Exp, scale=-1.0).then_inc(sem("eabs_ready"), 1)
                            act.wait_ge(sem("eabs_ready"), m + 1)
                            A(gt[:, :], gt[:, :], ACT.Ln, bias=1.0).then_inc(sem("ln_ready"), 1)
                        if c == s0 + 1:
                            act.wait_ge(sem("cs_ready"), 2 * m + 2)
                            if m > 0:
                                act.wait_ge(sem("pair_done"), m)
                            both = cs[:, :].rearrange("p (a b) -> p a b", a=2)
                            A(e_q[:, :, :], both, ACT.Exp, scale=1 / 16).then_inc(sem("expb_ready"), 1)
                            A(e_k[:, :, :], both, ACT.Exp, scale=-1 / 16).then_inc(sem("expb_ready"), 1)
                            act.wait_ge(sem("bdiff_ready"), 2 * m + 2)
                            A(e_e[:, :, :], e_e[:, :, :], ACT.Exp, scale=1 / 16).then_inc(sem("expe_ready"), 1)
                        if c == s0 + 4:
                            act.wait_ge(sem("keT_psum"), m + 1)
                            if m > 0:
                                act.wait_ge(sem("kv_done"), m)
                            copy(keT[:, :, :], pt[:, :].rearrange("p (a b) -> p a b", a=4), "keT_ready")
                        if c == s0 + GLA_OUT:
                            act.wait_ge(sem("pair_done"), m + 1)
                            copy(o[:, 2 * pr, :], pn[:, 0:T], "o_gla")
                            copy(o[:, 2 * pr + 1, :], ps[:, 0:T], "o_gla")
                    for pr in range(PAIRS):
                        if c == GLAN_AT + pr:
                            act.wait_ge(sem("osq_used"), 16 * l + 2 + 2 * pr)
                            root((pt, ps, pt)[pr][:, :], 0, 2 * T, P, 7 * l + 2 + pr)
                    if c == CONVN_AT:
                        act.wait_ge(sem("osq_used"), 16 * l + 10)
                        root(pn[:, 0:T], 0, T, CONVT * P, 7 * l + 5)
                    if c == MLAN_AT:
                        act.wait_ge(sem("osq_used"), 16 * l + 16)
                        root(pn[:, 0:T], 0, T, HEADS * P, 7 * l + 6)
                    part = c - FIRST_CHUNK["z3"] - 1
                    if 0 <= part < 3:
                        y_hi(l, part)
                    if part == 2:
                        y_hi(l, 3)
                    if name[:3] == "out" and k == 3:
                        for j in range(4):
                            square_x(16 * (l + 1) + 4 * i + j)
                    if c + 1 < NC:
                        for m in range(ada_before(l, c) // 4, ada_before(l, c + 1) // 4):
                            ada_rows(ADA_FIRST[l] // 4 + m)
                    if h_due(l, c):
                        for t in range(c + 1, c + 5):
                            h_hi(l, t)
                act.wait_ge(sem("xsq_used"), 16 * (l + 2))
                root(ps[:, 0:T], 0, T, D, 7 * (l + 1))

        @block.tensor
        def _(pe):
            def ada_chunk(n):
                l, g, k = ADA[n]
                landed(pe, "a", n)
                if k == 0 and n >= 4:
                    pe.wait_ge(sem("ada_biased"), n // 4)
                for r in range(ROWS):
                    mm = pe.matmul(pa[32 * r:32 * r + 32, :], cz[:, ROWS * k + r, :],
                                   ring[:, slot("a", n), r * WIDE:(r + 1) * WIDE],
                                   start=(k == 0), stop=(k == 3))
                mm.then_inc(sem("ada_used"), 1)

            def ada_turn(m):
                pe.wait_ge(sem("arow_ready"), m + 1)
                for j in range(4):
                    mm = pe.transpose(pa[:, j * P:(j + 1) * P], arow[:, j * P:(j + 1) * P], ident)
                mm.then_inc(sem("ada_turned"), 1)

            def xsum(m):
                pe.wait_ge(sem("xsq_ready"), m + 1)
                mm = pe.matmul(ps[:, 0:T], ones, sqx[:, m % 4, :], start=(m % 16 == 0), stop=(m % 16 == 15))
                mm.then_inc(sem("xsq_used"), 1)

            def wait_evacuated(n):
                l, g = divmod(n, len(PP_GROUPS))
                name = PP_GROUPS[g]
                i = int(name[-1]) if name[-1].isdigit() else 0
                if name == "latq":
                    pe.wait_ge(sem("lat_ready"), 3 * l + 2)
                elif name == "latkv":
                    pe.wait_ge(sem("lat_ready"), 3 * l + 3)
                elif name[:2] == "uq":
                    pe.wait_ge(sem("qn_ready"), 6 * l + 2 * i + 2)
                elif name[:2] == "kn":
                    pe.wait_ge(sem("kn_ready"), 6 * l + 3 * i + 3)
                elif name[:2] == "vm":
                    pe.wait_ge(sem("vm_ready"), 4 * l + 2 * i + 2)
                elif name[:2] == "gv":
                    pe.wait_ge(sem("gv_ready"), 4 * l + 2 * i + 2)
                elif name[:4] == "conv":
                    pe.wait_ge(sem("o_conv"), 4 * l + i + 1)
                elif name[0] == "z":
                    pe.wait_ge(sem("silu_ready"), 8 * l + 2 * i + 2)
                else:
                    pe.wait_ge(sem("x_ready"), 16 * l + 4 * i + 4)

            def weight_chunk(l, c):
                g, k = CHUNKS[c]
                name, cols, kt, nch = GROUPS[g]
                n = chunk_no(l, c)
                s = n % SPLIT
                pe.wait_ge(sem("lo_ready"), n + 1)
                if k == 0 and name in PP_GROUPS and pp_no(l, name) >= 2:
                    wait_evacuated(pp_no(l, name) - 2)
                if name[:2] in ("uq", "kn", "vm"):
                    base, mv_hi, mv_lo = 0 if name[:2] == "uq" else 3, lat_hi, lat_lo
                    pe.wait_ge(sem("latlo_ready"), 5 * (l + 1))
                else:
                    base, mv_hi, mv_lo = ROWS * k, a_hi, a_lo
                for r in range(kt):
                    if name == "latq":
                        pe.wait_ge(sem("hlo_ready"), 16 * l + base + r + 1)
                    if name == "out0":
                        pe.wait_ge(sem("ylo_ready"), 8 * l + (base + r) // 2 + 1)
                    hi_w = w_hi[:, s, r * cols:(r + 1) * cols]
                    lo_w = w_lo[:, s, r * cols:(r + 1) * cols]
                    first, last = k == 0 and r == 0, k == nch - 1 and r == kt - 1
                    if name[:2] in ("vm", "gv"):
                        for j in range(2):
                            ah = mv_hi[:, base + r, j * P:(j + 1) * P]
                            al = mv_lo[:, base + r, j * P:(j + 1) * P]
                            to = gbanks(l, name)[j][:, 0:cols]
                            pe.matmul(to, ah, hi_w, start=first, stop=False)
                            pe.matmul(to, ah, lo_w, start=False, stop=False)
                            mm = pe.matmul(to, al, hi_w, start=False, stop=last)
                    else:
                        for j in range(cols // P):
                            to = tile_of(l, name, j)
                            hi_j, lo_j = hi_w[:, j * P:(j + 1) * P], lo_w[:, j * P:(j + 1) * P]
                            ah, al = mv_hi[:, base + r, :], mv_lo[:, base + r, :]
                            pe.matmul(to, hi_j, ah, start=first and opens_bank(name, j), stop=False,
                                      skip_group_check=True)
                            pe.matmul(to, hi_j, al, start=False, stop=False, skip_group_check=True)
                            mm = pe.matmul(to, lo_j, ah, start=False, stop=last, skip_group_check=True)
                mm.then_inc(sem("chunk_done"), 1)

            def kv(bk, col, d, n, hh, pr):
                r = (n % 2) * CH
                h = 2 * pr + hh
                return pe.matmul(bk[hh * DK:(hh + 1) * DK, col * P:(col + 1) * P],
                                 keT[r:r + CH, d * 2 + n // 2, hh * DK:(hh + 1) * DK],
                                 gv[r:r + CH, n // 2, h * P:(h + 1) * P], start=True, stop=True)

            def osums(n0, count, to, first, last):
                for i in range(count):
                    pe.wait_ge(sem("osq_ready"), n0 + i + 1)
                    pe.matmul(to(i), ones, sqo[:, (n0 + i) % 4, :], start=first(i), stop=last(i)
                              ).then_inc(sem("osq_used"), 1)

            pe.wait_ge(sem("const_in"), 16)
            pe.wait_ge(sem("cz_ready"), 1)
            for l in range(DEPTH):
                for n in range(ada_before(l, 0)):
                    if l == 0 or n >= 2:
                        ada_chunk(ADA_FIRST[l] + n)
                    if n % 4 == 3:
                        ada_turn((ADA_FIRST[l] + n) // 4)
                    if l == 0 and n == 3:
                        for m in range(16):
                            xsum(m)
                        pe.wait_ge(sem("wg_in"), 16)
                for c, (g, k) in enumerate(CHUNKS):
                    name = GROUPS[g][0]
                    weight_chunk(l, c)
                    for m in turns_in(l, c):
                        ada_turn(ADA_FIRST[l] // 4 + m)
                    if c == LAT_AT:
                        pe.wait_ge(sem("gqk_ready"), 6 * (l + 1))
                        for i in range(5):
                            pe.wait_ge(sem("latsq_ready"), 5 * l + i + 1)
                            pe.matmul(pn[:, (i // 3) * T:(i // 3) * T + T], ones, sqx[:, i % 4, :],
                                      start=i in (0, 3), stop=i in (2, 4)).then_inc(sem("latsq_used"), 1)
                    h = c - MLA_AT - 2
                    if 0 <= h < HEADS:
                        pe.wait_ge(sem("probT_ready"), HEADS * l + h + 1)
                        if h > 0:
                            pe.wait_ge(sem("o_mla"), HEADS * l + h)
                        else:
                            pe.wait_ge(sem("root_ready"), 8 * l + 7)
                        for kt in range(2):
                            mm = pe.matmul(pn[:, 0:T], vm[:, kt, h * P:(h + 1) * P],
                                           probT[:, kt * T:(kt + 1) * T], start=(kt == 0), stop=(kt == 1))
                        mm.then_inc(sem("pv_done"), 1)
                    h = c - MLA_AT - 1
                    if 0 <= h < HEADS:
                        pe.wait_ge(sem("probn_ready"), 2 * (HEADS * l + h) + 2)
                        if h > 0:
                            pe.wait_ge(sem("probT_ready"), HEADS * l + h)
                        else:
                            pe.wait_ge(sem("root_ready"), 8 * l + 6)
                        for kt in range(2):
                            for q in range(2):
                                mm = pe.transpose(pt[:, kt * T + q * P:kt * T + (q + 1) * P],
                                                  prob[:, q, kt * P:(kt + 1) * P], ident)
                        mm.then_inc(sem("prob_used"), 1)
                    h = c - MLA_AT
                    if 0 <= h < HEADS:
                        if h == 0:
                            pe.wait_ge(sem("root_ready"), 8 * l + 5)
                            pe.wait_ge(sem("kr_ready"), 2 * (l + 1))
                            pe.wait_ge(sem("qr_ready"), 3 * (l + 1))
                            pe.wait_ge(sem("qn_ready"), 6 * (l + 1))
                            pe.wait_ge(sem("kn_ready"), 6 * (l + 1))
                            pe.wait_ge(sem("vm_ready"), 4 * (l + 1))
                        else:
                            pe.wait_ge(sem("exp_ready"), 2 * (HEADS * l + h))
                        r = (h % 2) * DK
                        for q in range(2):
                            to = ps[:, q * T:(q + 1) * T]
                            pe.matmul(to, o[:, 6 + h, q * P:(q + 1) * P], kn[:, h, :], start=True, stop=False)
                            mm = pe.matmul(to, qr[r:r + DK, h // 2, q * P:(q + 1) * P], kr[r:r + DK, :],
                                           start=False, stop=True)
                        mm.then_inc(sem("score_ready"), 1)
                    for pr in range(PAIRS):
                        s0 = GLA_AT + GLA_STEPS * pr
                        m = PAIRS * l + pr
                        if c == s0 - 1:
                            pe.wait_ge(sem("lr_ready"), l + 1)
                            if pr == 0:
                                pe.wait_ge(sem("root_ready"), 8 * l + 3)
                            else:
                                pe.wait_ge(sem("gx_ready"), 2 * m)
                            if pr > 1:
                                pe.wait_ge(sem("o_gla"), HEADS * l + 2 * (pr - 1))
                            for d in range(2):
                                mm = pe.matmul(pn[:, d * T:(d + 1) * T],
                                               wgs[DK:P, l, d * QL + pr * P:d * QL + (pr + 1) * P], lrT[DK:P, :],
                                               start=True, stop=True)
                            mm.then_inc(sem("gate_psum"), 1)
                        if c == s0 + 3:
                            pe.wait_ge(sem("qdec_ready"), 2 * m + 2)
                            pe.wait_ge(sem("kinv_ready"), m + 1)
                            if pr > 0:
                                pe.wait_ge(sem("sta_ready"), 6 * m)
                                pe.wait_ge(sem("o_gla"), HEADS * l + 2 * pr)
                            for hh in range(2):
                                rows = slice(hh * DK, (hh + 1) * DK)
                                for d in range(2):
                                    for tt in range(2):
                                        tok = slice(tt * P, (tt + 1) * P)
                                        mm = pe.matmul((ps, pt)[hh][:, (d * 2 + tt) * P:(d * 2 + tt + 1) * P],
                                                       e_k[rows, d, tok], e_q[rows, d, tok], start=True, stop=True)
                                mm.then_inc(sem("gscore_ready"), 1)
                        if c == s0 + 4:
                            pe.wait_ge(sem("kend_ready"), m + 1)
                            pe.wait_ge(sem("st_ready"), 4 * m + 4)
                            for d in range(2):
                                for tt in range(2):
                                    mm = pe.transpose(pt[:, (d * 2 + tt) * P:(d * 2 + tt + 1) * P],
                                                      e_e[:, d, tt * P:(tt + 1) * P], ident)
                            mm.then_inc(sem("keT_psum"), 1)
                        if c == s0 + 5:
                            pe.wait_ge(sem("keT_ready"), m + 1)
                            pe.wait_ge(sem("gv_ready"), 4 * l + (2 if pr == 0 else 4))
                            for col, (d, n) in enumerate([(0, 0), (0, 2), (1, 2)]):
                                for hh in range(2):
                                    kv(ps, col, d, n, hh, pr)
                            for col, (d, n) in enumerate([(0, 1), (1, 3), (1, 1)]):
                                for hh in range(2):
                                    mm = kv(pt, col, d, n, hh, pr)
                            mm.then_inc(sem("kv_done"), 1)
                        if c == s0 + GLA_OUT:
                            pe.wait_ge(sem("sta_ready"), 6 * m + 6)
                            if pr + 1 < PAIRS:
                                pe.wait_ge(sem("gx_ready"), 2 * m + 4)
                            for hh in range(2):
                                bk = (pn, ps)[hh]
                                h = 2 * pr + hh
                                rows = slice(hh * DK, (hh + 1) * DK)
                                for tt in range(2):
                                    pe.matmul(bk[:, tt * P:(tt + 1) * P], gv[:, tt, h * P:(h + 1) * P],
                                              st[:, hh, tt, :], start=(tt == 0), stop=False, skip_group_check=True)
                                for d in range(2):
                                    for i in range(3):
                                        n = i + 1 if d == 0 else 2 - i
                                        mm = pe.matmul(bk[:, n * CH:(n + 1) * CH], sta[rows, d, i, :],
                                                       e_q[rows, d, n * CH:(n + 1) * CH], start=False,
                                                       stop=(d == 1 and i == 2), skip_group_check=True)
                            mm.then_inc(sem("pair_done"), 1)
                    for pr in range(PAIRS):
                        if c == GLAN_AT + pr:
                            bk = (pt, ps, pt)[pr]
                            if pr == 0:
                                pe.wait_ge(sem("sta_ready"), 6 * PAIRS * (l + 1))
                            if pr == 1:
                                pe.wait_ge(sem("o_gla"), HEADS * (l + 1))
                            if pr == 2:
                                pe.wait_ge(sem("root_ready"), 8 * l + 4)
                            osums(16 * l + 2 * pr, 2, lambda i: bk[:, i * T:(i + 1) * T],
                                  lambda i: True, lambda i: True)
                    if c == CONVN_AT:
                        pe.wait_ge(sem("o_gla"), HEADS * (l + 1))
                        osums(16 * l + 6, 4, lambda i: pn[:, 0:T], lambda i: i == 0, lambda i: i == 3)
                    if c == MLAN_AT:
                        pe.wait_ge(sem("o_mla"), HEADS * (l + 1))
                        osums(16 * l + 10, 6, lambda i: pn[:, 0:T], lambda i: i == 0, lambda i: i == 5)
                    if c + 1 == NC and l + 1 < DEPTH:
                        for n in range(2):
                            ada_chunk(ADA_FIRST[l + 1] + n)
                    if name[:3] == "out" and k == 3:
                        if name == "out0":
                            pe.wait_ge(sem("exp_ready"), 2 * HEADS * (l + 1))
                        for j in range(4):
                            xsum(16 * (l + 1) + 4 * int(name[3]) + j)
                    if c + 1 < NC:
                        for n in range(ada_before(l, c), ada_before(l, c + 1)):
                            ada_chunk(ADA_FIRST[l] + n)
                    if h_due(l, c):
                        ada_turn(ADA_FIRST[l] // 4 + ada_before(l, c + 1) // 4 - 1)

        @block.vector
        def _(dve):
            told = {}

            def tell(ins, name):
                ins.then_inc(sem(name), 1)
                told[name] = told.get(name, 0) + 1
                told["last"] = name

            def own(name):
                dve.wait_ge(sem(name), told[name])

            def settle():
                own(told["last"])

            def split_lo(n):
                l, c = divmod(n, NC)
                cols = GROUPS[CHUNKS[c][0]][1] * GROUPS[CHUNKS[c][0]][2]
                dve.wait_ge(sem("hi_ready"), n + 1)
                tell(dve.tensor_tensor(w_lo[:, n % SPLIT, 0:cols], ring[:, slot("w", n), 0:cols],
                                       w_hi[:, n % SPLIT, 0:cols], ALU.subtract), "lo_ready")

            def ada_bias(m):
                l, g, _ = ADA[4 * m]
                dve.wait_ge(sem("ada_turned"), m + 1)
                tell(dve.tensor_reduce(asum[:, :], pa[:, :].rearrange("p (j r e) -> p j r e", j=4, e=32)[:, :, :, 0],
                                       AX.X, ALU.add), "ada_read")
                own("ada_read")
                tell(dve.tensor_tensor(acol[:, l, 4 * g:4 * g + 4], asum[:, :], p(l, C_ADAB + 4 * g, 4),
                                       ALU.add), "ada_biased")

            def invert(roots, to):
                settle()
                dve.wait_ge(sem("root_ready"), roots)
                tell(dve.reciprocal(to, rs[:, 0:to.shape[1]]), "rinv_ready")
                own("rinv_ready")

            def h_part(l, part):
                settle()
                four = slice(4 * part, 4 * part + 4)
                tell(dve.scalar_tensor_tensor(hscale[:, four], acol[:, l, 16 + 4 * part:20 + 4 * part], 1.0,
                                              p(l, C_NORM + 4 * part, 4), ALU.add, ALU.mult), "shift_ready")
                own("shift_ready")
                for t in range(4 * part, 4 * part + 4):
                    tell(dve.scalar_tensor_tensor(tmp[:, t % 4, :], x[:, t, :], hscale[:, t:t + 1],
                                                  rstd[:, :], ALU.mult, ALU.mult), "hmul_ready")
                for t in range(4 * part, 4 * part + 4):
                    dve.wait_ge(sem("ahi_ready"), 16 * l + t + 1)
                    tell(dve.scalar_tensor_tensor(a_lo[:, t, :], tmp[:, t % 4, :], acol[:, l, t:t + 1],
                                                  a_hi[:, t, :], ALU.add, ALU.subtract), "hlo_ready")

            def rope(src, rows, dst, done):
                settle()
                tell(dve.tensor_tensor(ropet[0:rows, 0, :], src[0:rows, :], rope_cos[0:rows, :], ALU.mult),
                     "rope_part")
                for r in range(0, rows, 32):
                    other = r + 32 if r % 64 == 0 else r - 32
                    tell(dve.tensor_tensor(ropet[r:r + 32, 1, :], src[other:other + 32, :],
                                           rope_sin[other:other + 32, :], ALU.mult),
                         "rope_used" if r + 32 == rows else "rope_part")
                settle()
                for at in range(0, P, rows):
                    tell(dve.tensor_tensor(dst[at:at + rows, :], ropet[0:rows, 0, :], ropet[0:rows, 1, :], ALU.add),
                         done)

            dve.wait_ge(sem("const_in"), 16)
            dve.wait_ge(sem("pos_in"), 16)

            def chain(ins):
                tell(ins, "setup")
                own("setup")

            chain(dve.tensor_copy(ang[:, 0:T], pos_i[:, :]))
            chain(dve.tensor_scalar(ang[:, 0:T], ang[:, 0:T], kst[:, K_FREQ:K_FREQ + 1], None, ALU.mult))
            chain(dve.tensor_copy(ang[:, T:2 * T], ang[:, 0:T]))
            chain(dve.tensor_scalar(turns[:, 0:T], ang[:, 0:T], 0.15915494309189535, 0.25, ALU.mult, ALU.add))
            chain(dve.tensor_scalar(turns[:, T:2 * T], ang[:, 0:T], 0.15915494309189535, None, ALU.mult))
            chain(dve.tensor_scalar(turns[:, :], turns[:, :], MAGIC, None, ALU.add))
            chain(dve.tensor_scalar(turns[:, :], turns[:, :], MAGIC, None, ALU.subtract))
            for part in TWO_PI:
                chain(dve.scalar_tensor_tensor(ang[:, :], turns[:, :], -part, ang[:, :], ALU.mult, ALU.add))
            chain(dve.tensor_scalar(ang[:, 0:T], ang[:, 0:T], 1.5707963267948966, None, ALU.add))
            tell(dve.tensor_scalar(ang[:, 0:T], ang[:, 0:T], 3.1415925, -3.1415925, ALU.min, ALU.max),
                 "angle_ready")
            tell(dve.tensor_scalar(ang[:, T:2 * T], ang[:, T:2 * T], 3.1415925, -3.1415925, ALU.min, ALU.max),
                 "angle_ready")
            dve.wait_ge(sem("trig"), 2)
            chain(dve.tensor_scalar(rope_sin[:, :], rope_sin[:, :], kst[:, K_SIGN:K_SIGN + 1], None, ALU.mult))
            dve.wait_ge(sem("par_in"), 16)
            dve.wait_ge(sem("x_in"), 16)
            dve.wait_ge(sem("fin_in"), 16)
            dve.wait_ge(sem("u_zero"), 1)
            dve.wait_ge(sem("st_zero"), 1)
            invert(1, rstd[:, :])
            split_lo(0)

            for l in range(DEPTH):
                for m in range(ada_before(l, 0) // 4):
                    if l == 0:
                        ada_bias(m)
                h_part(l, 0)
                for m in range(ada_before(l, 0) // 4):
                    if l > 0:
                        ada_bias(ADA_FIRST[l] // 4 + m)
                for c, (g, k) in enumerate(CHUNKS):
                    n = chunk_no(l, c)
                    if n + 1 < DEPTH * NC:
                        split_lo(n + 1)
                    for m in turns_in(l, c):
                        ada_bias(ADA_FIRST[l] // 4 + m)
                    if l > 0 and c % 4 == 2 and c < 12:
                        h_part(l, c // 4 + 1)
                    name = GROUPS[g][0]
                    if k == GROUPS[g][3] - 1:
                        if name == "latq":
                            dve.wait_ge(sem("chunk_done"), n + 1)
                            rope(tile_of(l, name, 0), DK, kr, "kr_ready")
                        elif name[:2] == "uq":
                            dve.wait_ge(sem("chunk_done"), n + 1)
                            rope(tile_of(l, name, 1), P, qr[:, int(name[2]), :], "qr_ready")
                        elif name[:4] == "conv":
                            i = int(name[4])
                            settle()
                            dve.wait_ge(sem("cc_ready"), 4 * l + i + 1)
                            tell(dve.tensor_tensor(u[:, 1:T + 1], tile_of(l, name, 1), ccs[:, :], ALU.mult), "u_ready")
                            own("u_ready")
                            tell(dve.tensor_scalar(cv[:, 0, :], u[:, 0:T], p(l, C_CW + i), None, ALU.mult), "tap")
                            own("tap")
                            tell(dve.scalar_tensor_tensor(cv[:, 1, :], u[:, 1:T + 1], p(l, C_CW + 4 + i),
                                                          cv[:, 0, :], ALU.mult, ALU.add), "tap")
                            own("tap")
                            tell(dve.scalar_tensor_tensor(cv[:, 0, :], u[:, 2:T + 2], p(l, C_CW + 8 + i),
                                                          cv[:, 1, :], ALU.mult, ALU.add), "tap")
                            own("tap")
                            tell(dve.tensor_tensor(o[:, 12 + i, :], tile_of(l, name, 2), cv[:, 0, :], ALU.mult),
                                 "o_conv")
                        elif name[:3] == "out":
                            i = int(name[3])
                            settle()
                            dve.wait_ge(sem("chunk_done"), n + 1)
                            for j in range(4):
                                t = 4 * i + j
                                tell(dve.scalar_tensor_tensor(x[:, t, :], tile_of(l, name, j), acol[:, l, 32 + t:33 + t],
                                                              x[:, t, :], ALU.mult, ALU.add), "x_ready")
                    if c == LAT_AT + 1:
                        invert(8 * l + 3, rinv[:, :])
                        for i in range(5):
                            half = (i // 3) * T
                            gain = p(l, C_QG + i) if i < 3 else p(l, C_KVG + i - 3)
                            tell(dve.scalar_tensor_tensor(lat[:, i, :], lat[:, i, :], gain,
                                                          rinv[:, half:half + T], ALU.mult, ALU.mult),
                                 "latn_ready")
                        for i in range(5):
                            dve.wait_ge(sem("lathi_ready"), 5 * l + i + 1)
                            tell(dve.tensor_tensor(lat_lo[:, i, :], lat[:, i, :], lat_hi[:, i, :],
                                                   ALU.subtract), "latlo_ready")
                    h = c - MLA_AT
                    if 0 <= h < HEADS:
                        settle()
                        dve.wait_ge(sem("score_ready"), HEADS * l + h + 1)
                        tell(dve.tensor_reduce(mx[:, :], ps[:, :].rearrange("p (a b) -> p a b", a=2), AX.X,
                                               ALU.max), "mx_ready")
                        own("mx_ready")
                        tell(dve.tensor_scalar(nmx[:, :], mx[:, :], -SM_SCALE, None, ALU.mult), "nmx_ready")
                        dve.wait_ge(sem("exp_ready"), 2 * (HEADS * l + h) + 2)
                        tell(dve.reciprocal(rsi[:, :], rsum[:, :]), "rsi_ready")
                        own("rsi_ready")
                        for q in range(2):
                            tell(dve.tensor_scalar(prob[:, q, :], prob[:, q, :], rsi[:, q:q + 1], None, ALU.mult),
                                 "probn_ready")
                    for pr in range(PAIRS):
                        s0 = GLA_AT + GLA_STEPS * pr
                        m = PAIRS * l + pr
                        if c == s0:
                            settle()
                            dve.wait_ge(sem("gate_psum"), m + 1)
                            for d in range(2):
                                tell(dve.tensor_scalar(gx[:, d * T:(d + 1) * T], pn[:, d * T:(d + 1) * T],
                                                       p(l, (C_BGF, C_BGB)[d] + pr), None, ALU.add), "gx_ready")
                        if c == s0 + 1:
                            settle()
                            dve.wait_ge(sem("ln_ready"), m + 1)
                            tell(dve.scalar_tensor_tensor(gx[:, :], gx[:, :], 0.0, gt[:, :], ALU.min,
                                                          ALU.subtract), "la_ready")
                            own("la_ready")
                            scan = kst[:, K_SCAN:K_SCAN + T]
                            tell(dve.tensor_tensor_scan(cs[:, 0:T], scan, gx[:, 0:T], 0.0, ALU.mult, ALU.add),
                                 "cs_ready")
                            tell(dve.tensor_tensor_scan(cs[:, 2 * T - 1:T - 1:-1], scan, gx[:, 2 * T - 1:T - 1:-1],
                                                        0.0, ALU.mult, ALU.add), "cs_ready")
                            own("cs_ready")
                            if m:
                                dve.wait_ge(sem("keT_psum"), m)
                            for d in range(2):
                                b = cs[:, d * T:(d + 1) * T].rearrange("p (n s) -> p n s", n=NCH)
                                end = b[:, :, CH - 1:CH] if d == 0 else b[:, :, 0:1]
                                tell(dve.tensor_tensor(e_e[:, d, :].rearrange("p (n s) -> p n s", n=NCH),
                                                       end.to_broadcast([P, NCH, CH]), b, ALU.subtract),
                                     "bdiff_ready")
                        if c == s0 + 2:
                            settle()
                            dve.wait_ge(sem("expb_ready"), 2 * m + 2)
                            for d in range(2):
                                b = e_q[:, d, :].rearrange("p (n s) -> p n s", n=NCH)
                                end = b[:, :, CH - 1] if d == 0 else b[:, :, 0]
                                tell(dve.tensor_copy(dec[:, d, :], end), "dec_ready")
                            own("dec_ready")
                            for d in range(2):
                                tell(dve.scalar_tensor_tensor(e_q[:, d, :], o[:, 2 * pr, :], DK ** -0.5,
                                                              e_q[:, d, :], ALU.mult, ALU.mult), "qdec_ready")
                        if c == s0 + 3:
                            settle()
                            if m:
                                dve.wait_ge(sem("pair_done"), m)
                            for d, mask in enumerate((K_MF, K_MB)):
                                if d:
                                    settle()
                                for hh in range(2):
                                    dve.wait_ge(sem("gscore_ready"), 2 * m + hh + 1)
                                    tell(dve.copy_predicated(
                                        st[:, hh, :, :].rearrange("p a b -> p (a b)"),
                                        kst[:, mask:mask + T].bitcast(I32),
                                        (ps, pt)[hh][:, d * T:(d + 1) * T]), "st_ready")
                        if c == s0 + 5:
                            settle()
                            dve.wait_ge(sem("kv_done"), m + 1)
                            even = lambda i: ps[:, i * P:(i + 1) * P]
                            odd = lambda i: pt[:, i * P:(i + 1) * P]
                            tell(dve.tensor_copy(sta[:, 0, 0, :], even(0)), "sta_ready")
                            tell(dve.tensor_copy(sta[:, 1, 0, :], odd(1)), "sta_ready")
                            own("sta_ready")
                            tell(dve.scalar_tensor_tensor(sta[:, 0, 1, :], sta[:, 0, 0, :], dec[:, 0, 1:2],
                                                          odd(0), ALU.mult, ALU.add), "sta_ready")
                            tell(dve.scalar_tensor_tensor(sta[:, 1, 1, :], sta[:, 1, 0, :], dec[:, 1, 2:3],
                                                          even(2), ALU.mult, ALU.add), "sta_ready")
                            own("sta_ready")
                            tell(dve.scalar_tensor_tensor(sta[:, 0, 2, :], sta[:, 0, 1, :], dec[:, 0, 2:3],
                                                          even(1), ALU.mult, ALU.add), "sta_ready")
                            tell(dve.scalar_tensor_tensor(sta[:, 1, 2, :], sta[:, 1, 1, :], dec[:, 1, 1:2],
                                                          odd(2), ALU.mult, ALU.add), "sta_ready")
                    for pr in range(PAIRS):
                        if c == GLAN_AT + pr:
                            invert(8 * l + 4 + pr, rinv[:, :])
                            two = o[:, 2 * pr:2 * pr + 2, :].rearrange("p a b -> p (a b)")
                            tell(dve.scalar_tensor_tensor(two, two, p(l, C_GLAG), rinv[:, :], ALU.mult, ALU.mult),
                                 "onorm_gla")
                    if c == CONVN_AT:
                        invert(8 * l + 7, rinv[:, 0:T])
                        for i in range(4):
                            tell(dve.scalar_tensor_tensor(o[:, 12 + i, :], o[:, 12 + i, :], p(l, C_CG + i),
                                                          rinv[:, 0:T], ALU.mult, ALU.mult), "onorm_conv")
                    if c == MLAN_AT:
                        invert(8 * l + 8, rinv[:, 0:T])
                        for i in range(6):
                            tell(dve.scalar_tensor_tensor(o[:, 6 + i, :], o[:, 6 + i, :], p(l, C_MLAG + i),
                                                          rinv[:, 0:T], ALU.mult, ALU.mult), "onorm_mla")
                    part = c - FIRST_CHUNK["z3"] - 1
                    for q in ([part, 3] if part == 2 else [part] if 0 <= part < 2 else []):
                        for t in (4 * q, 4 * q + 2):
                            dve.wait_ge(sem("yhi_ready"), 8 * l + t // 2 + 1)
                            tell(dve.tensor_tensor(a_lo[:, t:t + 2, :], o[:, Y_ORDER[t]:Y_ORDER[t] + 2, :],
                                                   a_hi[:, t:t + 2, :], ALU.subtract), "ylo_ready")
                    if h_due(l, c):
                        ada_bias(ADA_FIRST[l] // 4 + ada_before(l, c + 1) // 4 - 1)
                        h_part(l, c // 4 + 1)
                invert(8 * (l + 1) + 1, rstd[:, :])
            for t in range(KT):
                tell(dve.scalar_tensor_tensor(o[:, t, :], x[:, t, :], fing[:, t:t + 1], rstd[:, :],
                                              ALU.mult, ALU.mult), "final_ready")


def pack_stream(w_in, w_out, w_uq, w_ukv):
    import numpy as np
    at = np.cumsum([0, 384, 384, 768, 32, 384, 256, 64, 512, 512, 512, 2048])
    gq, gk, gv, lr, mq, mkv, mkr, cb, cc, cx, z = (np.arange(a, b) for a, b in zip(at[:-1], at[1:]))
    small_tile = -np.ones(P, int)
    small_tile[0:64], small_tile[64:80], small_tile[96:112] = mkr, lr[0:16], lr[16:32]
    head = lambda h, w: np.arange(w * h, w * (h + 1))
    cols = {"latq": np.concatenate([small_tile, mq]), "latkv": mkv, "gq": gq, "gk": gk}
    for i in range(3):
        a, b = head(2 * i, 192), head(2 * i + 1, 192)
        cols[f"uq{i}"] = np.concatenate([a[:128], a[128:], b[128:], b[:128]])
    for i in range(2):
        cols[f"kn{i}"] = np.concatenate([head(h, 256)[:128] for h in range(3 * i, 3 * i + 3)])
        cols[f"vm{i}"] = np.concatenate([head(h, 256)[128:] for h in range(3 * i, 3 * i + 3)])
        cols[f"gv{i}"] = gv[384 * i:384 * i + 384]
    for i in range(CONVT):
        s = slice(P * i, P * i + P)
        cols[f"conv{i}"] = np.concatenate([cc[s], cx[s], cb[s]])
    for i in range(4):
        cols[f"z{i}"] = np.concatenate([z[P * t:P * t + P] for t in Y_ORDER[4 * i:4 * i + 4]])
        cols[f"out{i}"] = np.arange(512 * i, 512 * i + 512)
    y_rows = np.concatenate([np.arange(P * t, P * t + P) for t in Y_ORDER])
    out = np.zeros((DEPTH, STREAM_AT[-1]), w_in.dtype)
    for l in range(DEPTH):
        for c, (g, k) in enumerate(CHUNKS):
            name, width, kt, _ = GROUPS[g]
            src = w_uq[l] if name[:2] == "uq" else w_ukv[l] if name[:2] in ("kn", "vm") else \
                w_out[l][y_rows] if name[:3] == "out" else w_in[l]
            rows = src[k * kt * P:(k + 1) * kt * P]
            part = np.where(cols[name] >= 0, rows[:, np.maximum(cols[name], 0)], np.zeros((), w_in.dtype))
            out[l, STREAM_AT[c]:STREAM_AT[c + 1]] = part.reshape(kt, P, width).transpose(1, 0, 2).ravel()
    return out


def kernel(**inputs):
    import numpy as np
    import concourse.bacc as _bacc
    from concourse import mybir as _mybir
    from concourse.bass_utils import run_bass_kernel_spmd as _run

    a = {k: np.asarray(v) for k, v in inputs.items()}
    f4 = np.float32

    def tiles(v):
        return np.swapaxes(v.reshape(*v.shape[:-1], -1, P), -1, -2)

    par = np.zeros((P, DEPTH, SMALL), f4)
    put = lambda col, v: par.__setitem__((slice(None), slice(None), slice(col, col + v.shape[-1])),
                                         np.moveaxis(v, 0, 1))
    put(C_NORM, tiles(a["norm_g"]))
    put(C_ADAB, tiles(a["ada_b"]))
    put(C_BGF, tiles(a["gla_bg_f"]))
    put(C_BGB, tiles(a["gla_bg_b"]))
    put(C_GLAG, tiles(a["gla_norm_g"]))
    put(C_QG, tiles(a["mla_q_norm_g"]))
    put(C_KVG, tiles(a["mla_kv_norm_g"]))
    put(C_MLAG, tiles(a["mla_out_g"]))
    for tap in range(3):
        put(C_CW + 4 * tap, tiles(a["conv_w"][:, tap]))
    put(C_CG, tiles(a["conv_out_g"]))
    wg = np.zeros((64, DEPTH, 2 * QL), f4)
    wg[0:RANK, :, 0:QL] = a["gla_wg_f"].transpose(1, 0, 2)
    wg[32:32 + RANK, :, QL:] = a["gla_wg_b"].transpose(1, 0, 2)

    const = np.zeros((P, CONST), f4)
    const[:, K_ONES:K_ONES + P] = 1
    const[:, K_ID:K_ID + P] = np.eye(P)
    j, i = np.arange(P)[:, None], np.arange(T)[None, :] % P
    same = j // CH == i // CH
    const[:, K_MF:K_MF + T] = same & (j <= i)
    const[:, K_MB:K_MB + T] = same & (j > i)
    const[:, K_SCAN:K_SCAN + T] = np.arange(T) % CH != 0
    const[:, K_SEL] = np.arange(P) % 32 == 0
    const[:, K_SIGN] = np.where(np.arange(P) % 64 < 32, 1, -1)
    const[:, K_FREQ] = np.float32(10000.0) ** (-(np.arange(P) % 32).astype(f4) * 2 / np.float32(64))
    const[:, K_EPS] = EPS

    ada = a["ada_w"].reshape(DEPTH, 4, ROWS, P, ADA_GROUPS, WIDE).transpose(0, 4, 1, 3, 2, 5)
    arrays = {
        "xT": np.ascontiguousarray(a["x"][0].T.reshape(KT, P, T).transpose(1, 0, 2)),
        "cT": np.ascontiguousarray(tiles(a["c"][0])),
        "posr": np.ascontiguousarray(a["positions"]),
        "wstream": pack_stream(a["w_in"], a["w_out"], a["mla_w_uq"], a["mla_w_ukv"]),
        "adastream": np.ascontiguousarray(ada).reshape(DEPTH, ADA_GROUPS, 4, P, ROWS * WIDE),
        "wg": wg, "small": par, "finalg": np.ascontiguousarray(tiles(a["final_g"])), "const": const,
    }
    nc = _bacc.Bacc("TRN2", target_bir_lowering=False, num_devices=1,
                     dynamic_dma_scratch_size=1024)
    aps = {n: nc.dram_tensor(n, v.shape, _mybir.dt.from_np(v.dtype), kind="ExternalInput").ap()
           for n, v in arrays.items()}
    out = nc.dram_tensor("out", (P, KT, T), _mybir.dt.float32, kind="ExternalOutput").ap()
    build(nc, out=out, **aps)
    r = _run(nc, [arrays], core_ids=[0]).results[0]["out"]
    return np.ascontiguousarray(r.transpose(1, 0, 2).reshape(D, T).T)[None]
```

```python
from contextlib import ExitStack

import concourse.bass as bass
from concourse import mybir

P = 128
D = 2048
T = 256
DEPTH = 2
KT = D // P
HEADS = 6
PAIRS = HEADS // 2
DK = 64
CH = 64
NCH = T // CH
RANK = 16
QL, KVL = 384, 256
CONVT = 4
EPS = 1e-6
ROWS = 4
RING, SPLIT = 4, 3
AHEAD = 2
WIDE = 512
ADA_GROUPS = 3 * D // WIDE
SM_SCALE = (128 + 64) ** -0.5

GROUPS = (
    [("latq", 512, ROWS, 4), ("latkv", 256, ROWS, 4), ("gq", 384, ROWS, 4), ("gk", 384, ROWS, 4)]
    + [(f"gv{i}", 384, ROWS, 4) for i in range(2)]
    + [g for i in range(3) for g in ((f"uq{i}", 384, 3, 1), (f"conv{i}", 384, ROWS, 4))]
    + [("kn0", 384, 2, 1), ("vm0", 384, 2, 1), ("conv3", 384, ROWS, 4), ("kn1", 384, 2, 1), ("vm1", 384, 2, 1)]
    + [(f"z{i}", 512, ROWS, 4) for i in range(4)]
    + [(f"out{i}", 512, ROWS, 4) for i in range(4)]
)
GROUP_AT = {g[0]: n for n, g in enumerate(GROUPS)}
SIDE = 4
CHUNKS = [(n, k) for k in range(4) for n in range(SIDE)] + [
    (n, k) for n, g in enumerate(GROUPS) if n >= SIDE for k in range(g[3])]
NC = len(CHUNKS)
FIRST_CHUNK = {g: min(i for i, (n, _) in enumerate(CHUNKS) if GROUPS[n][0] == g) for g in GROUP_AT}
LAST_CHUNK = {g: max(i for i, (n, _) in enumerate(CHUNKS) if GROUPS[n][0] == g) for g in GROUP_AT}
SIZES = [P * GROUPS[n][1] * GROUPS[n][2] for n, _ in CHUNKS]
STREAM_AT = [sum(SIZES[:i]) for i in range(NC + 1)]
Y_ORDER = [0, 1, 2, 3, 12, 13, 14, 15, 4, 5, 6, 7, 8, 9, 10, 11]

C_NORM, C_ADAB, C_BGF, C_BGB, C_GLAG, C_QG, C_KVG, C_MLAG, C_CW, C_CG = (
    0, 16, 64, 67, 70, 71, 74, 76, 82, 94)
SMALL = 98
K_ONES, K_ID, K_MF, K_MB, K_SCAN, K_SEL, K_SIGN, K_FREQ, K_EPS = 0, 128, 256, 512, 768, 1024, 1028, 1029, 1030
CONST = 1031

GATES_AT = LAST_CHUNK["gv0"]
SCAN_AT = GATES_AT + 1
GLA_AT = GATES_AT + 2
GLA_STEPS = 5
GLA_OUT = 5
GLAN_AT = GLA_AT + GLA_STEPS * (PAIRS - 1) + GLA_OUT + 1
CONVN_AT = LAST_CHUNK["conv3"] + 2
MLA_AT = LAST_CHUNK["vm1"] + 2
MLAN_AT = MLA_AT + HEADS + 3
PP_GROUPS = [g[0] for g in GROUPS if g[0] not in ("gq", "gk")]
LAT_AT = SIDE * 4
N_X, N_LAT, N_GLA, N_CONV, N_MLA, A_LAYER = 0, 1, 2, 5, 6, 7
NORMS = DEPTH * A_LAYER + 1
MAGIC = 1.5 * 2.0 ** 23
TWO_PI = (6.28125, 2029 / 2.0 ** 20, 6.283185307179586 - 6.28125 - 2029 / 2.0 ** 20)


def ada_bundles(layer):
    first = [([(0, j), (0, 4 + j)], "pe") for j in range(4)] if layer == 0 else []
    gates = [([(layer, g) for g in range(8, 12)], "pe")] if layer == 0 else [
        ([(layer, g)], "dve" if g > 8 else "pe") for g in range(8, 12)]
    after = [([(layer + 1, 0), (layer + 1, 1)], "pe")] + [([(layer + 1, g)], "dve") for g in range(2, 8)]
    return first + gates + (after if layer + 1 < DEPTH else [])


BUNDLES = [b for _l in range(DEPTH) for b, _ in ada_bundles(_l)]
BY = [who for _l in range(DEPTH) for _, who in ada_bundles(_l)]
GROUPS_BEFORE = [sum(len(b) for b in BUNDLES[:i]) for i in range(len(BUNDLES) + 1)]
ADA = [(b, i, k) for b in range(len(BUNDLES)) for i in range(len(BUNDLES[b])) for k in range(4)]
ADA_FIRST = [0]
for _l in range(DEPTH):
    ADA_FIRST.append(ADA_FIRST[-1] + sum(4 * len(b) for b, _ in ada_bundles(_l)))


def done_by(who, b):
    return BY[:b].count(who)


def chunk_count(who, n):
    return sum(BY[b] == who for b, _, _ in ADA[:n + 1])


def ada_before(layer, c):
    clip = lambda n, most: max(0, min(n, most))
    if layer:
        return 4 + clip(c - FIRST_CHUNK["z0"], ADA_FIRST[layer + 1] - ADA_FIRST[layer] - 4)
    if c <= 16:
        return 8 + 2 * min(c, 12) + (c % 4 == 0 and c < 12)
    return 32 + clip(c - 16, 16) + clip(c - 34, 8) + clip(c - FIRST_CHUNK["z0"], 15) + clip(c - FIRST_CHUNK["out0"], 9)


def boundary_bundle(l):
    return ADA[ADA_FIRST[l]][0]


def h_due(l, c):
    return l == 0 and c in (3, 7, 11)


def bundles_ended(l, c):
    if not 0 <= c < NC - 1:
        return []
    return [b for b in range(len(BUNDLES)) if 4 * GROUPS_BEFORE[b + 1] - 1 in ada_chunks(l, c)]


def bundles_due(l, c):
    return [b for who, lag in (("pe", 1), ("dve", 2)) if not h_due(l, c - lag)
            for b in bundles_ended(l, c - lag) if BY[b] == who]


def ada_chunks(l, c):
    return range(ADA_FIRST[l] + ada_before(l, c), ADA_FIRST[l] + ada_before(l, c + 1))


LOADS = []
for _l in range(DEPTH):
    LOADS += [("a", ADA_FIRST[_l] + n) for n in range(ada_before(_l, 0))]
    if _l == 0:
        LOADS.insert(6, ("w", 0))
        LOADS += [("w", n) for n in range(1, AHEAD)]
    for _c in range(NC):
        LOADS += [("w", _l * NC + _c + AHEAD)] if _l * NC + _c + AHEAD < DEPTH * NC else []
        if _c + 1 < NC:
            LOADS += [("a", n) for n in ada_chunks(_l, _c)]
PLACE = {key: i for i, key in enumerate(LOADS)}


def xsums_before(l, i):
    return 4 + 10 * l + 2 * i + 2 * (i == 4)


def build(nc, xT, cT, posr, wstream, adastream, wg, small, finalg, const, out):
    F32, F32R, I32 = mybir.dt.float32, mybir.dt.float32r, mybir.dt.int32
    ALU, ACT, AX = mybir.AluOpType, mybir.ActivationFunctionType, mybir.AxisListType
    with ExitStack() as ctx:
        def sb(name, shape, dt=F32):
            return ctx.enter_context(nc.sbuf_tensor(name, shape, dt))

        def bank(name):
            return ctx.enter_context(nc.psum_tensor(name, [P, 512], F32))

        sems = {}

        def sem(name):
            if name not in sems:
                sems[name] = ctx.enter_context(nc.semaphore(name))
            return sems[name]

        x = sb("x", [P, KT, T])
        a_hi = sb("a_hi", [P, KT, T], F32R)
        a_lo = sb("a_lo", [P, KT, T], F32R)
        o = sb("o", [P, KT, T])
        ring = sb("ring", [P, RING, ROWS * WIDE])
        w_hi = sb("w_hi", [P, SPLIT, ROWS * WIDE], F32R)
        w_lo = sb("w_lo", [P, SPLIT, ROWS * WIDE], F32R)
        arow = sb("arow", [P, WIDE])
        acc = sb("acc", [P, 2, WIDE])
        acol = sb("acol", [P, DEPTH, 48])
        hscale = sb("hscale", [P, KT])
        ct = sb("ct", [P, KT])
        cz = sb("cz", [P, KT, 35])
        kst = sb("kst", [P, CONST])
        par = sb("par", [P, DEPTH, SMALL])
        fing = sb("fing", [P, KT])
        wgs = sb("wgs", [P, DEPTH, 2 * QL])
        pos_i = sb("pos_i", [P, T], I32)
        rope_cos = sb("rope_cos", [P, T])
        rope_sin = sb("rope_sin", [P, T])
        sqx = sb("sqx", [P, 4, T])
        sqo = sqx
        rs = sb("rs", [P, NORMS, 4])
        rinv = sb("rinv", [P, NORMS, 4])
        rstd = sb("rstd", [P, T])
        tmp = sb("tmp", [P, 4, T])
        cs = sb("cs", [P, 2 * PAIRS, T])
        sz = tmp[:, :, :].rearrange("p (j a) b -> p j (a b)", j=2)
        lat = sb("lat", [P, HEADS, T])
        gv = lat[:, :, :].rearrange("p a b -> p (a b)").rearrange("p (j c) -> p j c", j=2)
        kn = lat
        lat_hi = sb("lat_hi", [P, 5, T], F32R)
        lat_lo = sb("lat_lo", [P, 5, T], F32R)
        kr = sb("kr", [P, T])
        qr = sb("qr", [P, PAIRS, T])
        cv = sb("cv", [P, 2, T])
        ropet = cv
        mx = sb("mx", [P, 2])
        nmx = sb("nmx", [P, 2])
        rsum = sb("rsum", [P, 2])
        rsi = sb("rsi", [P, 2])
        lrT = sb("lrT", [P, T])
        e_q = sb("e_q", [P, 2, T])
        e_k = sb("e_k", [P, 2, T])
        prob, probT = e_q, e_k[:, :, :].rearrange("p a b -> p (a b)")
        vm = sb("vm", [P, 2, HEADS * P])
        gla = vm[:, :, :].rearrange("p a b -> p (a b)")
        gt = gla[:, :]
        e_e = gla[:, 0:2 * T].rearrange("p (a b) -> p a b", a=2)
        keT = gla[:, 2 * T:4 * T].rearrange("p (a b) -> p a b", a=4)
        ang, turns = gla[:, 0:2 * T], gla[:, 2 * T:4 * T]
        dec = sb("dec", [P, 2, NCH])
        st = sb("st", [P, 2, 2, P])
        sta = sb("sta", [P, 2, 3, P])
        ccs = sb("ccs", [P, T])
        u = sb("u", [P, T + 2])

        pp = [bank(f"pp{i}") for i in range(4)]
        pa, ps, pt, pn = bank("pa"), bank("ps"), bank("pt"), bank("pn")

        ones, ident = kst[:, K_ONES:K_ONES + P], kst[:, K_ID:K_ID + P]
        eps = kst[:, K_EPS:K_EPS + 1]

        def chunk_no(l, c):
            return l * NC + c

        def tile_of(l, name, j):
            if name in ("gq", "gk"):
                half = j + 3 * (name == "gk")
                return (ps, pt, pn)[half // 2][:, (half % 2) * T:(half % 2) * T + T]
            return gbanks(l, name)[j // 2][:, (j % 2) * T:(j % 2) * T + T]

        def opens_bank(name, j):
            return (j + 3 * (name == "gk")) % 2 == 0

        def pp_no(l, name):
            return l * len(PP_GROUPS) + PP_GROUPS.index(name)

        def gbanks(l, name):
            n = pp_no(l, name)
            return pp[2 * (n % 2)], pp[2 * (n % 2) + 1]

        def p(l, col, n=1):
            return par[:, l, col:col + n]

        def slot(kind, n):
            return PLACE[kind, n] % RING

        def landed(eng, kind, n):
            i = PLACE[kind, n]
            eng.wait_ge(sem(f"ring_in{i % RING}"), 16 * (i // RING + 1))

        block = ctx.enter_context(nc.Block())

        @block.sync
        def _(sp):
            sp.dma_start(ct[:, :], cT).then_inc(sem("c_in"), 16)
            sp.dma_start(kst[:, :], const).then_inc(sem("const_in"), 16)
            sp.dma_start(pos_i[:, :], posr.partition_broadcast(P)).then_inc(sem("pos_in"), 16)
            sp.dma_start(par[:, :, :], small).then_inc(sem("par_in"), 16)
            for i, (kind, n) in enumerate(LOADS):
                if i >= RING:
                    before, m = LOADS[i - RING]
                    if before == "a" and BY[ADA[m][0]] == "pe":
                        sp.wait_ge(sem("ada_used"), chunk_count("pe", m))
                    elif before == "a":
                        sp.wait_ge(sem("ada_summed"), chunk_count("dve", m))
                    else:
                        sp.wait_ge(sem("lo_ready"), m + 1)
                if kind == "a":
                    b, at, k = ADA[n]
                    l, g = BUNDLES[b][at]
                    src, cols = adastream[l, g, k], ROWS * WIDE
                else:
                    l, c = divmod(n, NC)
                    cols = GROUPS[CHUNKS[c][0]][1] * GROUPS[CHUNKS[c][0]][2]
                    src = wstream[l, STREAM_AT[c]:STREAM_AT[c + 1]].rearrange("(p n) -> p n", p=P)
                sp.dma_start(ring[:, i % RING, 0:cols], src).then_inc(sem(f"ring_in{i % RING}"), 16)
                if i == RING - 1:
                    sp.dma_start(x[:, :, :], xT).then_inc(sem("x_in"), 16)
                if i == 32:
                    sp.dma_start(wgs[DK:P, :, :], wg).then_inc(sem("wg_in"), 16)
                    sp.dma_start(fing[:, :], finalg).then_inc(sem("fin_in"), 16)
            for q in range(4):
                sp.wait_ge(sem("final_ready"), q + 1)
                sp.dma_start(out[:, 4 * q:4 * q + 4, :], o[:, 4 * q:4 * q + 4, :]).then_inc(sem("out_done"), 16)
            sp.wait_ge(sem("out_done"), 16 * 4)

        @block.gpsimd
        def _(pool):
            pool.memset(cz[:, :, :], 0.0).then_inc(sem("cz_zero"), 1)
            pool.memset(st[:, :, :, :], 0.0).then_inc(sem("st_zero"), 1)
            pool.memset(u[:, :], 0.0).then_inc(sem("u_zero"), 1)

            parts = [0]

            def part(ins):
                ins.then_inc(sem("osq_part"), 1)
                parts[0] += 1
                pool.wait_ge(sem("osq_part"), parts[0])

            def gla_squares(l):
                for i in range(HEADS):
                    if i >= 4:
                        pool.wait_ge(sem("osq_used"), 8 * l + i - 3)
                    pool.wait_ge(sem("o_gla"), HEADS * l + i + 1)
                    pool.tensor_tensor(sqo[:, i % 4, :], o[:, i, :], o[:, i, :], ALU.mult
                                       ).then_inc(sem("osq_ready"), 1)

            def squares_sum(l, tiles, name, at):
                for i, t in enumerate(tiles):
                    pool.wait_ge(sem(name), len(tiles) * l + i + 1)
                    to = sqo[:, at + (i > 0), :]
                    part(pool.tensor_tensor(to, o[:, t, :], o[:, t, :], ALU.mult))
                    if 0 < i < len(tiles) - 1:
                        part(pool.tensor_tensor(sqo[:, at, :], sqo[:, at, :], to, ALU.add))
                pool.tensor_tensor(sqo[:, at, :], sqo[:, at, :], to, ALU.add).then_inc(sem("osq_ready"), 1)

            def gate_z(l, i):
                for j in range(2):
                    pool.wait_ge(sem("silu_ready"), 8 * l + 2 * i + j + 1)
                    t = Y_ORDER[4 * i + 2 * j]
                    if i == 0:
                        pool.wait_ge(sem("onorm_gla"), 3 * (l + 1))
                    elif i == 1:
                        pool.wait_ge(sem("onorm_conv"), 4 * (l + 1))
                    else:
                        pool.wait_ge(sem("onorm_mla"), 6 * (l + 1))
                    pool.tensor_tensor(o[:, t:t + 2, :], o[:, t:t + 2, :],
                                       sz[:, j, :].rearrange("p (a b) -> p a b", a=2), ALU.mult
                                       ).then_inc(sem("y_ready"), 1)

            for l in range(DEPTH):
                for pr in range(PAIRS):
                    m = PAIRS * l + pr
                    key = o[:, 2 * pr + 1:2 * pr + 2, :].to_broadcast([P, 2, T])
                    pool.wait_ge(sem("expb_ready"), 2 * m + 2)
                    pool.tensor_tensor(e_k[:, :, :], key, e_k[:, :, :], ALU.mult).then_inc(sem("kinv_ready"), 1)
                    pool.wait_ge(sem("expe_ready"), m + 1)
                    pool.tensor_tensor(e_e[:, :, :], key, e_e[:, :, :], ALU.mult).then_inc(sem("kend_ready"), 1)
                gla_squares(l)
                pool.wait_ge(sem("osq_used"), 8 * l + 4)
                squares_sum(l, range(12, 16), "o_conv", 2)
                gate_z(l, 0)
                pool.wait_ge(sem("osq_used"), 8 * l + 6)
                squares_sum(l, range(6, 12), "o_mla", 0)
                for i in range(1, 4):
                    gate_z(l, i)
                for i in range(3):
                    pool.wait_ge(sem("xsq_ready"), 16 * l + 4 * i + 4)
                    pool.tensor_tensor(sqx[:, 0:2, :], sqx[:, 0:2, :], sqx[:, 2:4, :], ALU.add
                                       ).then_inc(sem("xpair_ready"), 1)

        @block.scalar
        def _(act):
            A = act.activation

            def split_hi(n):
                g, _ = CHUNKS[n % NC]
                cols = GROUPS[g][1] * GROUPS[g][2]
                landed(act, "w", n)
                if n >= SPLIT:
                    act.wait_ge(sem("chunk_done"), n - SPLIT + 1)
                A(w_hi[:, n % SPLIT, 0:cols], ring[:, slot("w", n), 0:cols], ACT.Identity
                  ).then_inc(sem("hi_ready"), 1)

            def ada_rows(b):
                act.wait_ge(sem("ada_used"), chunk_count("pe", 4 * GROUPS_BEFORE[b + 1] - 1))
                if b:
                    act.wait_ge(sem("ada_turned"), b)
                A(arow[:, :], pa[:, :], ACT.Identity).then_inc(sem("arow_ready"), 1)

            def root(bk, norm, lo, hi, width):
                A(rs[:, norm, lo:hi], bk[:, lo:hi], ACT.Sqrt, bias=eps, scale=1.0 / width
                  ).then_inc(sem("root_ready"), 1)

            def h_hi(l, t):
                act.wait_ge(sem("hmul_ready"), 16 * l + t + 1)
                if t == 0 and l > 0:
                    act.wait_ge(sem("chunk_done"), chunk_no(l, 0))
                if t % 4 == 0:
                    act.wait_ge(sem("shift_ready"), 4 * l + t // 4 + 1)
                A(a_hi[:, t, :], tmp[:, t % 4, :], ACT.Identity, bias=acol[:, l, t:t + 1]
                  ).then_inc(sem("ahi_ready"), 1)

            def square_x(l, i):
                if i:
                    act.wait_ge(sem("xsq_used"), xsums_before(l, i))
                for j in range(4):
                    act.wait_ge(sem("x_ready"), 16 * l + 4 * i + j + 1)
                    A(sqx[:, j, :], x[:, 4 * i + j, :], ACT.Square).then_inc(sem("xsq_ready"), 1)

            def gain(i):
                act.wait_ge(sem("fin_in"), 16)
                for t in range(4 * i, 4 * i + 4):
                    A(o[:, t, :], x[:, t, :], ACT.Identity, scale=fing[:, t:t + 1]).then_inc(sem("gained"), 1)

            def y_hi(l, part):
                act.wait_ge(sem("chunk_done"), chunk_no(l, FIRST_CHUNK["z3"] + part) + 1)
                for t in (4 * part, 4 * part + 2):
                    act.wait_ge(sem("y_ready"), 8 * l + t // 2 + 1)
                    copy(a_hi[:, t:t + 2, :], o[:, Y_ORDER[t]:Y_ORDER[t] + 2, :], "yhi_ready")

            def copy(dst, src, done):
                A(dst, src, ACT.Identity).then_inc(sem(done), 1)

            act.wait_ge(sem("c_in"), 16)
            act.wait_ge(sem("cz_zero"), 1)
            A(cz[:, :, 3], ct[:, :], ACT.Silu).then_inc(sem("cz_ready"), 1)
            act.wait_ge(sem("angle_ready"), 2)
            A(rope_cos[:, :], ang[:, 0:T], ACT.Sin).then_inc(sem("trig"), 1)
            A(rope_sin[:, :], ang[:, T:2 * T], ACT.Sin).then_inc(sem("trig"), 1)
            act.wait_ge(sem("x_in"), 16)
            act.wait_ge(sem("const_in"), 16)
            for q in range(2):
                A(o[:, 8 * q:8 * q + 8, :], x[:, 8 * q:8 * q + 8, :], ACT.Square).then_inc(sem("x0sq_ready"), 1)
            act.wait_ge(sem("xsq_used"), 4)
            root(ps, N_X, 0, 2, D)
            for l in range(DEPTH):
                if l == 0:
                    split_hi(0)
                    ada_rows(0)
                for t in range(4):
                    h_hi(l, t)
                if l:
                    ada_rows(boundary_bundle(l))
                if l == 0:
                    for n in range(1, AHEAD):
                        split_hi(n)
                for c, (g, k) in enumerate(CHUNKS):
                    n = chunk_no(l, c)
                    if n + AHEAD < DEPTH * NC:
                        split_hi(n + AHEAD)
                    if l > 0 and c % 4 == 2 and c < 12:
                        for t in range(c + 2, c + 6):
                            h_hi(l, t)
                    name = GROUPS[g][0]
                    i = int(name[-1]) if name[-1].isdigit() else 0
                    if k == GROUPS[g][3] - 1 and name[:3] != "out":
                        act.wait_ge(sem("chunk_done"), n + 1)
                        if name == "latq":
                            b0, b1 = gbanks(l, name)
                            act.wait_ge(sem("rope_used"), 4 * l + 1)
                            copy(lrT[DK:P, :], b0[DK:P, 0:T], "lr_ready")
                            copy(lat[:, 0, :], b0[:, T:2 * T], "lat_ready")
                            copy(lat[:, 1:3, :], b1[:, :].rearrange("p (a b) -> p a b", a=2), "lat_ready")
                        elif name == "latkv":
                            copy(lat[:, 3:5, :], gbanks(l, name)[0][:, :].rearrange("p (a b) -> p a b", a=2),
                                 "lat_ready")
                        elif name == "gk":
                            for i in range(6):
                                copy(o[:, 2 * (i % 3) + i // 3, :], tile_of(l, ("gq", "gk")[i // 3], i % 3),
                                     "gqk_ready")
                        elif name[:2] == "uq":
                            act.wait_ge(sem("rope_used"), 4 * l + i + 2)
                            copy(o[:, 6 + 2 * i, :], tile_of(l, name, 0), "qn_ready")
                            copy(o[:, 7 + 2 * i, :], tile_of(l, name, 2), "qn_ready")
                        elif name[:2] == "kn":
                            for j in range(3):
                                copy(kn[:, 3 * i + j, :], tile_of(l, name, j), "kn_ready")
                        elif name[:2] in ("vm", "gv"):
                            dst, done = (vm, "vm_ready") if name[:2] == "vm" else (gv, "gv_ready")
                            if name == "gv0":
                                act.wait_ge(sem("latlo_ready"), 5 * (l + 1))
                            for j in range(2):
                                copy(dst[:, j, 384 * i:384 * i + 384], gbanks(l, name)[j][:, 0:384], done)
                        elif name[:4] == "conv":
                            if i + l > 0:
                                act.wait_ge(sem("u_ready"), 4 * l + i)
                            copy(ccs[:, :], tile_of(l, name, 0), "cc_ready")
                        elif name[0] == "z":
                            for j in range(2):
                                m = 8 * l + 2 * i + j
                                if m >= 2:
                                    act.wait_ge(sem("y_ready"), m - 1)
                                A(sz[:, j, :], gbanks(l, name)[j][:, :], ACT.Silu).then_inc(sem("silu_ready"), 1)
                    if c == LAT_AT:
                        act.wait_ge(sem("lat_ready"), 3 * (l + 1))
                        for i in range(5):
                            if i == 4:
                                act.wait_ge(sem("latsq_used"), 5 * l + 1)
                            A(sqx[:, i % 4, :], lat[:, i, :], ACT.Square).then_inc(sem("latsq_ready"), 1)
                        act.wait_ge(sem("latsq_used"), 5 * l + 5)
                        root(pn, A_LAYER * l + N_LAT, 0, 2, QL)
                        root(pn, A_LAYER * l + N_LAT, 2, 4, KVL)
                    if c == LAT_AT + 1:
                        for i in range(5):
                            act.wait_ge(sem("latn_ready"), 5 * l + i + 1)
                            copy(lat_hi[:, i, :], lat[:, i, :], "lathi_ready")
                    h = c - MLA_AT - 2
                    if 0 <= h < HEADS:
                        act.wait_ge(sem("pv_done"), HEADS * l + h + 1)
                        copy(o[:, 6 + h, :], pn[:, 0:T], "o_mla")
                    h = c - MLA_AT - 1
                    if 0 <= h < HEADS:
                        act.wait_ge(sem("prob_used"), HEADS * l + h + 1)
                        if l + h > 0:
                            act.wait_ge(sem("pv_done"), HEADS * l + h)
                        copy(probT[:, :], pt[:, :], "probT_ready")
                    h = c - MLA_AT
                    if 0 <= h < HEADS:
                        act.wait_ge(sem("nmx_ready"), HEADS * l + h + 1)
                        if l + h > 0:
                            act.wait_ge(sem("prob_used"), HEADS * l + h)
                        for q in range(2):
                            A(prob[:, q, :], ps[:, q * T:q * T + T], ACT.Exp, bias=nmx[:, q:q + 1],
                              scale=SM_SCALE, accum_out=rsum[:, q:q + 1]).then_inc(sem("exp_ready"), 1)
                    if c == GATES_AT:
                        act.wait_ge(sem("gx_ready"), 6 * (l + 1))
                        A(gt, cs[:, :, :].rearrange("p a b -> p (a b)"), ACT.Abs).then_inc(sem("abs_ready"), 1)
                        act.wait_ge(sem("abs_ready"), l + 1)
                        A(gt, gt, ACT.Exp, scale=-1.0).then_inc(sem("eabs_ready"), 1)
                    if c == GATES_AT + 1:
                        act.wait_ge(sem("eabs_ready"), l + 1)
                        A(gt, gt, ACT.Ln, bias=1.0).then_inc(sem("ln_ready"), 1)
                    for pr in range(PAIRS):
                        s0 = GLA_AT + GLA_STEPS * pr
                        m = PAIRS * l + pr
                        if c == s0:
                            act.wait_ge(sem("cs_ready"), 6 * l + 2 * pr + 2)
                            if m > 0:
                                act.wait_ge(sem("pair_done"), m)
                            both = cs[:, 2 * pr:2 * pr + 2, :]
                            A(e_q[:, :, :], both, ACT.Exp, scale=1 / 16).then_inc(sem("expb_ready"), 1)
                            A(e_k[:, :, :], both, ACT.Exp, scale=-1 / 16).then_inc(sem("expb_ready"), 1)
                            act.wait_ge(sem("bdiff_ready"), 2 * m + 2)
                            A(e_e[:, :, :], e_e[:, :, :], ACT.Exp, scale=1 / 16).then_inc(sem("expe_ready"), 1)
                        if c == s0 + 3:
                            act.wait_ge(sem("keT_psum"), m + 1)
                            if m > 0:
                                act.wait_ge(sem("kv_done"), m)
                            copy(keT[:, :, :], pt[:, :].rearrange("p (a b) -> p a b", a=4), "keT_ready")
                        if c == s0 + GLA_OUT:
                            act.wait_ge(sem("pair_done"), m + 1)
                            copy(o[:, 2 * pr, :], pn[:, 0:T], "o_gla")
                            copy(o[:, 2 * pr + 1, :], ps[:, 0:T], "o_gla")
                    for pr in range(PAIRS):
                        if c == GLAN_AT + pr:
                            act.wait_ge(sem("osq_used"), 8 * l + 2 + 2 * pr)
                            root((pt, ps, pt)[pr], A_LAYER * l + N_GLA + pr, 0, 4, P)
                    if c == CONVN_AT:
                        act.wait_ge(sem("osq_used"), 8 * l + 7)
                        root(pn, A_LAYER * l + N_CONV, 0, 2, CONVT * P)
                    if c == MLAN_AT:
                        act.wait_ge(sem("osq_used"), 8 * l + 8)
                        root(pn, A_LAYER * l + N_MLA, 0, 2, HEADS * P)
                    part = c - FIRST_CHUNK["z3"] - 1
                    if 0 <= part < 3:
                        y_hi(l, part)
                    if part == 2:
                        y_hi(l, 3)
                    if name == "out3" and k == 0:
                        A(rs[:, NORMS - 1, 3:4], eps, ACT.Sqrt)
                    if name[:3] == "out" and k == 3:
                        square_x(l, i)
                        if l + 1 == DEPTH and i < 3:
                            gain(i)
                    for b in bundles_ended(l, c):
                        if BY[b] == "pe":
                            ada_rows(b)
                    if h_due(l, c):
                        for t in range(c + 1, c + 5):
                            h_hi(l, t)
                act.wait_ge(sem("xsq_used"), xsums_before(l, 4))
                root(ps, A_LAYER * (l + 1), 0, 2, D)
                if l + 1 == DEPTH:
                    gain(3)

        @block.tensor
        def _(pe):
            def ada_chunk(n):
                b, at, k = ADA[n]
                landed(pe, "a", n)
                opens, closes = at == 0 and k == 0, at + 1 == len(BUNDLES[b]) and k == 3
                if opens and b:
                    pe.wait_ge(sem("ada_biased"), GROUPS_BEFORE[b])
                for r in range(ROWS):
                    mm = pe.matmul(pa[32 * r:32 * r + 32, :], cz[:, ROWS * k + r, 3 - at:35 - at],
                                   ring[:, slot("a", n), r * WIDE:(r + 1) * WIDE], start=opens, stop=closes)
                mm.then_inc(sem("ada_used"), 1)

            def ada_turn(b):
                if BY[b] == "dve":
                    pe.wait_ge(sem("ada_summed"), 4 * done_by("dve", b) + 4)
                    pe.wait_ge(sem("ada_biased"), GROUPS_BEFORE[b])
                    for j in range(4):
                        mm = pe.matmul(pa[:, j:j + 1], acc[:, done_by("dve", b) % 2, j * P:(j + 1) * P], ones[:, 0:1],
                                       start=True, stop=True)
                    mm.then_inc(sem("ada_turned"), 1)
                    return
                pe.wait_ge(sem("arow_ready"), done_by("pe", b) + 1)
                size = len(BUNDLES[b])
                for j in range(4):
                    mm = pe.matmul(pa[:, j * size:(j + 1) * size], arow[:, j * P:(j + 1) * P],
                                   kst[:, K_SEL:K_SEL + size], start=True, stop=True)
                mm.then_inc(sem("ada_turned"), 1)

            def token_sums(bk, col, squares, first, last, opens=True):
                for tt in range(2):
                    mm = pe.matmul(bk[:, col + tt:col + tt + 1], squares[:, tt * P:(tt + 1) * P], ones[:, 0:1],
                                   start=first and opens and tt == 0, stop=last, skip_group_check=True)
                return mm

            def spread(bk, norm, cols):
                pe.wait_ge(sem("rinv_ready"), norm + 1)
                for j in range(cols):
                    mm = pe.matmul(bk[:, j * P:(j + 1) * P], rinv[:, norm, j:j + 1].to_broadcast([P, P]), ident,
                                   start=True, stop=True)
                mm.then_inc(sem("spread_done"), 1)

            def xsum(l, i):
                for j in range(2 if i < 3 else 4):
                    if i < 3:
                        pe.wait_ge(sem("xpair_ready"), 3 * l + i + 1)
                    else:
                        pe.wait_ge(sem("xsq_ready"), 16 * l + 12 + j + 1)
                    token_sums(ps, 0, sqx[:, j, :], i == 0 and j == 0, i == 3 and j == 3
                               ).then_inc(sem("xsq_used"), 1)

            def wait_evacuated(n):
                l, g = divmod(n, len(PP_GROUPS))
                name = PP_GROUPS[g]
                i = int(name[-1]) if name[-1].isdigit() else 0
                if name == "latq":
                    pe.wait_ge(sem("lat_ready"), 3 * l + 2)
                elif name == "latkv":
                    pe.wait_ge(sem("lat_ready"), 3 * l + 3)
                elif name[:2] == "uq":
                    pe.wait_ge(sem("qn_ready"), 6 * l + 2 * i + 2)
                elif name[:2] == "kn":
                    pe.wait_ge(sem("kn_ready"), 6 * l + 3 * i + 3)
                elif name[:2] == "vm":
                    pe.wait_ge(sem("vm_ready"), 4 * l + 2 * i + 2)
                elif name[:2] == "gv":
                    pe.wait_ge(sem("gv_ready"), 4 * l + 2 * i + 2)
                elif name[:4] == "conv":
                    pe.wait_ge(sem("o_conv"), 4 * l + i + 1)
                elif name[0] == "z":
                    pe.wait_ge(sem("silu_ready"), 8 * l + 2 * i + 2)
                else:
                    pe.wait_ge(sem("x_ready"), 16 * l + 4 * i + 4)

            def weight_chunk(l, c):
                g, k = CHUNKS[c]
                name, cols, kt, nch = GROUPS[g]
                n = chunk_no(l, c)
                s = n % SPLIT
                pe.wait_ge(sem("lo_ready"), n + 1)
                if k == 0 and name in PP_GROUPS and pp_no(l, name) >= 2:
                    wait_evacuated(pp_no(l, name) - 2)
                if name == "gq" and k == 0:
                    pe.wait_ge(sem("rstd_ready"), l + 1)
                if name[:2] in ("uq", "kn", "vm"):
                    base, mv_hi, mv_lo = 0 if name[:2] == "uq" else 3, lat_hi, lat_lo
                    pe.wait_ge(sem("latlo_ready"), 5 * (l + 1))
                else:
                    base, mv_hi, mv_lo = ROWS * k, a_hi, a_lo
                halves = [(0, 2), (2, 4)] if name[:3] == "out" and k == 3 else [(0, cols // P)]
                for (j0, j1), r in [(half, r) for half in halves for r in range(kt)]:
                    if name == "latq":
                        pe.wait_ge(sem("hlo_ready"), 16 * l + base + r + 1)
                    if name == "out0" and j0 == 0:
                        pe.wait_ge(sem("ylo_ready"), 8 * l + (base + r) // 2 + 1)
                    hi_w = w_hi[:, s, r * cols:(r + 1) * cols]
                    lo_w = w_lo[:, s, r * cols:(r + 1) * cols]
                    first, last = k == 0 and r == 0, k == nch - 1 and r == kt - 1
                    if name[:2] in ("vm", "gv"):
                        for j in range(2):
                            ah = mv_hi[:, base + r, j * P:(j + 1) * P]
                            al = mv_lo[:, base + r, j * P:(j + 1) * P]
                            to = gbanks(l, name)[j][:, 0:cols]
                            pe.matmul(to, ah, hi_w, start=first, stop=False)
                            pe.matmul(to, ah, lo_w, start=False, stop=False)
                            mm = pe.matmul(to, al, hi_w, start=False, stop=last)
                    else:
                        for j in range(j0, j1):
                            to = tile_of(l, name, j)
                            hi_j, lo_j = hi_w[:, j * P:(j + 1) * P], lo_w[:, j * P:(j + 1) * P]
                            ah, al = mv_hi[:, base + r, :], mv_lo[:, base + r, :]
                            pe.matmul(to, hi_j, ah, start=first and opens_bank(name, j), stop=False,
                                      skip_group_check=True)
                            pe.matmul(to, hi_j, al, start=False, stop=False, skip_group_check=True)
                            mm = pe.matmul(to, lo_j, ah, start=False, stop=last, skip_group_check=True)
                    if len(halves) == 2 and j1 == 2 and last:
                        mm.then_inc(sem("half_done"), 1)
                mm.then_inc(sem("chunk_done"), 1)

            def kv(bk, col, d, n, hh, pr):
                r = (n % 2) * CH
                h = 2 * pr + hh
                return pe.matmul(bk[hh * DK:(hh + 1) * DK, col * P:(col + 1) * P],
                                 keT[r:r + CH, d * 2 + n // 2, hh * DK:(hh + 1) * DK],
                                 gv[r:r + CH, n // 2, h * P:(h + 1) * P], start=True, stop=True)

            def osums(bk, n, slots):
                for i, at in enumerate(slots):
                    pe.wait_ge(sem("osq_ready"), n + i + 1)
                    token_sums(bk, 2 * i, sqo[:, at, :], True, True, i == 0).then_inc(sem("osq_used"), 1)

            pe.wait_ge(sem("const_in"), 16)
            pe.wait_ge(sem("cz_ready"), 1)
            for l in range(DEPTH):
                if l:
                    for n in range(2, 4):
                        ada_chunk(ADA_FIRST[l] + n)
                    spread(ps, A_LAYER * l, 2)
                for n in range(ada_before(l, 0) if l == 0 else 0):
                    ada_chunk(n)
                    if n == 5:
                        pe.wait_ge(sem("x0_ready"), 1)
                        for j in range(4):
                            token_sums(ps, 0, o[:, j, :], j == 0, j == 3).then_inc(sem("xsq_used"), 1)
                    if n == 6:
                        spread(ps, A_LAYER * l, 2)
                    if n == 7:
                        ada_turn(0)
                for c, (g, k) in enumerate(CHUNKS):
                    name = GROUPS[g][0]
                    weight_chunk(l, c)
                    if c == LAT_AT:
                        pe.wait_ge(sem("gqk_ready"), 6 * (l + 1))
                        for i in range(5):
                            pe.wait_ge(sem("latsq_ready"), 5 * l + i + 1)
                            token_sums(pn, 2 * (i // 3), sqx[:, i % 4, :], i in (0, 3), i in (2, 4), i == 0
                                       ).then_inc(sem("latsq_used"), 1)
                    if c == LAT_AT + 1:
                        spread(pn, A_LAYER * l + N_LAT, 4)
                    h = c - MLA_AT - 2
                    if 0 <= h < HEADS:
                        pe.wait_ge(sem("probT_ready"), HEADS * l + h + 1)
                        if h > 0:
                            pe.wait_ge(sem("o_mla"), HEADS * l + h)
                        else:
                            pe.wait_ge(sem("onorm_conv"), 4 * (l + 1))
                        for kt in range(2):
                            mm = pe.matmul(pn[:, 0:T], vm[:, kt, h * P:(h + 1) * P],
                                           probT[:, kt * T:(kt + 1) * T], start=(kt == 0), stop=(kt == 1))
                        mm.then_inc(sem("pv_done"), 1)
                    h = c - MLA_AT - 1
                    if 0 <= h < HEADS:
                        pe.wait_ge(sem("probn_ready"), 2 * (HEADS * l + h) + 2)
                        if h > 0:
                            pe.wait_ge(sem("probT_ready"), HEADS * l + h)
                        else:
                            pe.wait_ge(sem("onorm_gla"), 3 * (l + 1))
                        for kt in range(2):
                            for q in range(2):
                                mm = pe.transpose(pt[:, kt * T + q * P:kt * T + (q + 1) * P],
                                                  prob[:, q, kt * P:(kt + 1) * P], ident)
                        mm.then_inc(sem("prob_used"), 1)
                    h = c - MLA_AT
                    if 0 <= h < HEADS:
                        if h == 0:
                            pe.wait_ge(sem("onorm_gla"), 3 * l + 2)
                            pe.wait_ge(sem("kr_ready"), 2 * (l + 1))
                            pe.wait_ge(sem("qr_ready"), 3 * (l + 1))
                            pe.wait_ge(sem("qn_ready"), 6 * (l + 1))
                            pe.wait_ge(sem("kn_ready"), 6 * (l + 1))
                            pe.wait_ge(sem("vm_ready"), 4 * (l + 1))
                        else:
                            pe.wait_ge(sem("exp_ready"), 2 * (HEADS * l + h))
                        r = (h % 2) * DK
                        for q in range(2):
                            to = ps[:, q * T:(q + 1) * T]
                            pe.matmul(to, o[:, 6 + h, q * P:(q + 1) * P], kn[:, h, :], start=True, stop=False)
                            mm = pe.matmul(to, qr[r:r + DK, h // 2, q * P:(q + 1) * P], kr[r:r + DK, :],
                                           start=False, stop=True)
                        mm.then_inc(sem("score_ready"), 1)
                    if c == GATES_AT - 1:
                        pe.wait_ge(sem("wg_in"), 16)
                        pe.wait_ge(sem("lr_ready"), l + 1)
                        pe.wait_ge(sem("latn_ready"), 5 * (l + 1))
                        for pr in range(PAIRS):
                            for d in range(2):
                                mm = pe.matmul((ps, pt, pn)[pr][:, d * T:(d + 1) * T],
                                               wgs[DK:P, l, d * QL + pr * P:d * QL + (pr + 1) * P], lrT[DK:P, :],
                                               start=True, stop=True)
                        mm.then_inc(sem("gate_psum"), 1)
                    for pr in range(PAIRS):
                        s0 = GLA_AT + GLA_STEPS * pr
                        m = PAIRS * l + pr
                        if c == s0 + 2:
                            pe.wait_ge(sem("qdec_ready"), 2 * m + 2)
                            pe.wait_ge(sem("kinv_ready"), m + 1)
                            if pr > 0:
                                pe.wait_ge(sem("sta_ready"), 6 * m)
                                pe.wait_ge(sem("o_gla"), HEADS * l + 2 * pr)
                            for hh in range(2):
                                rows = slice(hh * DK, (hh + 1) * DK)
                                for d in range(2):
                                    for tt in range(2):
                                        tok = slice(tt * P, (tt + 1) * P)
                                        mm = pe.matmul((ps, pt)[hh][:, (d * 2 + tt) * P:(d * 2 + tt + 1) * P],
                                                       e_k[rows, d, tok], e_q[rows, d, tok], start=True, stop=True)
                                mm.then_inc(sem("gscore_ready"), 1)
                        if c == s0 + 3:
                            pe.wait_ge(sem("kend_ready"), m + 1)
                            pe.wait_ge(sem("st_ready"), 4 * m + 4)
                            for d in range(2):
                                for tt in range(2):
                                    mm = pe.transpose(pt[:, (d * 2 + tt) * P:(d * 2 + tt + 1) * P],
                                                      e_e[:, d, tt * P:(tt + 1) * P], ident)
                            mm.then_inc(sem("keT_psum"), 1)
                        if c == s0 + 4:
                            pe.wait_ge(sem("keT_ready"), m + 1)
                            pe.wait_ge(sem("gv_ready"), 4 * l + (2 if pr == 0 else 4))
                            for col, (d, n) in enumerate([(0, 0), (0, 2), (1, 2)]):
                                for hh in range(2):
                                    kv(ps, col, d, n, hh, pr)
                            for col, (d, n) in enumerate([(0, 1), (1, 3), (1, 1)]):
                                for hh in range(2):
                                    mm = kv(pt, col, d, n, hh, pr)
                            mm.then_inc(sem("kv_done"), 1)
                        if c == s0 + GLA_OUT:
                            pe.wait_ge(sem("sta_ready"), 6 * m + 6)
                            for hh in range(2):
                                bk = (pn, ps)[hh]
                                h = 2 * pr + hh
                                rows = slice(hh * DK, (hh + 1) * DK)
                                for tt in range(2):
                                    pe.matmul(bk[:, tt * P:(tt + 1) * P], gv[:, tt, h * P:(h + 1) * P],
                                              st[:, hh, tt, :], start=(tt == 0), stop=False, skip_group_check=True)
                                for d in range(2):
                                    for i in range(3):
                                        n = i + 1 if d == 0 else 2 - i
                                        mm = pe.matmul(bk[:, n * CH:(n + 1) * CH], sta[rows, d, i, :],
                                                       e_q[rows, d, n * CH:(n + 1) * CH], start=False,
                                                       stop=(d == 1 and i == 2), skip_group_check=True)
                            mm.then_inc(sem("pair_done"), 1)
                    for pr in range(PAIRS):
                        if c == GLAN_AT + pr:
                            bk = (pt, ps, pt)[pr]
                            if pr == 0:
                                pe.wait_ge(sem("sta_ready"), 6 * PAIRS * (l + 1))
                            if pr == 1:
                                pe.wait_ge(sem("o_gla"), HEADS * (l + 1))
                            if pr == 2:
                                pe.wait_ge(sem("onorm_gla"), 3 * l + 1)
                            osums(bk, 8 * l + 2 * pr, [2 * (pr % 2), 2 * (pr % 2) + 1])
                        if c == GLAN_AT + pr + 1:
                            spread((pt, ps, pt)[pr], A_LAYER * l + N_GLA + pr, 4)
                    if c == CONVN_AT:
                        pe.wait_ge(sem("o_gla"), HEADS * (l + 1))
                        osums(pn, 8 * l + 6, [2])
                    if c == CONVN_AT + 1:
                        spread(pn, A_LAYER * l + N_CONV, 2)
                    if c == MLAN_AT:
                        pe.wait_ge(sem("o_mla"), HEADS * (l + 1))
                        osums(pn, 8 * l + 7, [0])
                    if c == MLAN_AT + 1:
                        spread(pn, A_LAYER * l + N_MLA, 2)
                    if name in ("out1", "out2", "out3") and k == 1:
                        if name == "out1":
                            pe.wait_ge(sem("exp_ready"), 2 * HEADS * (l + 1))
                        xsum(l, int(name[3]) - 1)
                    if c + 1 == NC:
                        if l + 1 < DEPTH:
                            for n in range(2):
                                ada_chunk(ADA_FIRST[l + 1] + n)
                        xsum(l, 3)
                    if l and c == 0:
                        ada_turn(boundary_bundle(l))
                    for b in bundles_due(l, c):
                        ada_turn(b)
                    if c + 1 < NC:
                        for n in ada_chunks(l, c):
                            if BY[ADA[n][0]] == "pe":
                                ada_chunk(n)
                            if h_due(l, c) and n % 8 == 7:
                                ada_turn(bundles_ended(l, c)[0])
            spread(ps, A_LAYER * DEPTH, 2)

        @block.vector
        def _(dve):
            told = {}

            def tell(ins, name):
                ins.then_inc(sem(name), 1)
                told[name] = told.get(name, 0) + 1
                told["last"] = name

            def own(name):
                dve.wait_ge(sem(name), told[name])

            def settle():
                own(told["last"])

            def split_lo(n):
                l, c = divmod(n, NC)
                cols = GROUPS[CHUNKS[c][0]][1] * GROUPS[CHUNKS[c][0]][2]
                dve.wait_ge(sem("hi_ready"), n + 1)
                tell(dve.tensor_tensor(w_lo[:, n % SPLIT, 0:cols], ring[:, slot("w", n), 0:cols],
                                       w_hi[:, n % SPLIT, 0:cols], ALU.subtract), "lo_ready")

            def ada_bias(b):
                dve.wait_ge(sem("ada_turned"), b + 1)
                size = len(BUNDLES[b])
                for i, (l, g) in enumerate(BUNDLES[b]):
                    tell(dve.tensor_tensor(acol[:, l, 4 * g:4 * g + 4],
                                           pa[:, 0:4 * size].rearrange("p (j i) -> p j i", i=size)[:, :, i],
                                           p(l, C_ADAB + 4 * g, 4), ALU.add), "ada_biased")

            def ada_sum(n):
                b, _, k = ADA[n]
                to = acc[:, done_by("dve", b) % 2, :]
                landed(dve, "a", n)
                for r in range(ROWS):
                    src, by = ring[:, slot("a", n), r * WIDE:(r + 1) * WIDE], cz[:, ROWS * k + r, 3:4]
                    if k == 0 and r == 0:
                        dve.wait_ge(sem("ada_turned"), b - 1)
                        tell(dve.tensor_scalar(to, src, by, None, ALU.mult), "ada_part")
                    else:
                        settle()
                        tell(dve.scalar_tensor_tensor(to, src, by, to, ALU.mult, ALU.add),
                             "ada_part" if r + 1 < ROWS else "ada_summed")

            def invert(norm, cols):
                l, k = divmod(norm, A_LAYER)
                dve.wait_ge(sem("root_ready"), 8 * l + k + 1 + (k >= N_LAT))
                tell(dve.reciprocal(rinv[:, norm, 0:cols], rs[:, norm, 0:cols]), "rinv_ready")

            def spread(norm):
                settle()
                dve.wait_ge(sem("spread_done"), norm + 1)

            def h_part(l, part):
                settle()
                src = rstd[:, :] if part else ps[:, 0:T]
                four = slice(4 * part, 4 * part + 4)
                tell(dve.scalar_tensor_tensor(hscale[:, four], acol[:, l, 16 + 4 * part:20 + 4 * part], 1.0,
                                              p(l, C_NORM + 4 * part, 4), ALU.add, ALU.mult), "shift_ready")
                own("shift_ready")
                if part == 0:
                    dve.wait_ge(sem("spread_done"), A_LAYER * l + N_X + 1)
                for t in range(4 * part, 4 * part + 4):
                    tell(dve.scalar_tensor_tensor(tmp[:, t % 4, :], x[:, t, :], hscale[:, t:t + 1],
                                                  src, ALU.mult, ALU.mult), "hmul_ready")
                for t in range(4 * part, 4 * part + 4):
                    dve.wait_ge(sem("ahi_ready"), 16 * l + t + 1)
                    tell(dve.scalar_tensor_tensor(a_lo[:, t, :], tmp[:, t % 4, :], acol[:, l, t:t + 1],
                                                  a_hi[:, t, :], ALU.add, ALU.subtract), "hlo_ready")

            def rope(src, rows, dst, done):
                settle()
                tell(dve.tensor_tensor(ropet[0:rows, 0, :], src[0:rows, :], rope_cos[0:rows, :], ALU.mult),
                     "rope_part")
                for r in range(0, rows, 32):
                    other = r + 32 if r % 64 == 0 else r - 32
                    tell(dve.tensor_tensor(ropet[r:r + 32, 1, :], src[other:other + 32, :],
                                           rope_sin[other:other + 32, :], ALU.mult),
                         "rope_used" if r + 32 == rows else "rope_part")
                settle()
                for at in range(0, P, rows):
                    tell(dve.tensor_tensor(dst[at:at + rows, :], ropet[0:rows, 0, :], ropet[0:rows, 1, :], ALU.add),
                         done)

            dve.wait_ge(sem("const_in"), 16)
            dve.wait_ge(sem("pos_in"), 16)

            def chain(ins):
                tell(ins, "setup")
                own("setup")

            chain(dve.tensor_copy(ang[:, 0:T], pos_i[:, :]))
            chain(dve.tensor_scalar(ang[:, 0:T], ang[:, 0:T], kst[:, K_FREQ:K_FREQ + 1], None, ALU.mult))
            chain(dve.tensor_copy(ang[:, T:2 * T], ang[:, 0:T]))
            chain(dve.tensor_scalar(turns[:, 0:T], ang[:, 0:T], 0.15915494309189535, 0.25, ALU.mult, ALU.add))
            chain(dve.tensor_scalar(turns[:, T:2 * T], ang[:, 0:T], 0.15915494309189535, None, ALU.mult))
            chain(dve.tensor_scalar(turns[:, :], turns[:, :], MAGIC, None, ALU.add))
            chain(dve.tensor_scalar(turns[:, :], turns[:, :], MAGIC, None, ALU.subtract))
            for part in TWO_PI:
                chain(dve.scalar_tensor_tensor(ang[:, :], turns[:, :], -part, ang[:, :], ALU.mult, ALU.add))
            chain(dve.tensor_scalar(ang[:, 0:T], ang[:, 0:T], 1.5707963267948966, None, ALU.add))
            tell(dve.tensor_scalar(ang[:, 0:T], ang[:, 0:T], 3.1415925, -3.1415925, ALU.min, ALU.max),
                 "angle_ready")
            tell(dve.tensor_scalar(ang[:, T:2 * T], ang[:, T:2 * T], 3.1415925, -3.1415925, ALU.min, ALU.max),
                 "angle_ready")
            dve.wait_ge(sem("trig"), 2)
            chain(dve.tensor_scalar(rope_sin[:, :], rope_sin[:, :], kst[:, K_SIGN:K_SIGN + 1], None, ALU.mult))
            dve.wait_ge(sem("par_in"), 16)
            dve.wait_ge(sem("x_in"), 16)
            dve.wait_ge(sem("u_zero"), 1)
            dve.wait_ge(sem("st_zero"), 1)
            dve.wait_ge(sem("x0sq_ready"), 2)
            chain(dve.tensor_tensor(o[:, 0:8, :], o[:, 0:8, :], o[:, 8:16, :], ALU.add))
            tell(dve.tensor_tensor(o[:, 0:4, :], o[:, 0:4, :], o[:, 4:8, :], ALU.add), "x0_ready")
            dve.wait_ge(sem("cz_ready"), 1)
            invert(N_X, 2)

            for l in range(DEPTH):
                if l == 0:
                    split_lo(0)
                    ada_bias(0)
                h_part(l, 0)
                tell(dve.tensor_copy(rstd[:, :], ps[:, 0:T]), "rstd_ready")
                if l == 0:
                    for n in range(1, AHEAD):
                        split_lo(n)
                for c, (g, k) in enumerate(CHUNKS):
                    n = chunk_no(l, c)
                    if n + AHEAD < DEPTH * NC:
                        split_lo(n + AHEAD)
                    if l and c == 1:
                        ada_bias(boundary_bundle(l))
                    for b in bundles_due(l, c - 1):
                        ada_bias(b)
                    if l > 0 and c % 4 == 2 and c < 12:
                        h_part(l, c // 4 + 1)
                    name = GROUPS[g][0]
                    if k == GROUPS[g][3] - 1:
                        if name == "latq":
                            dve.wait_ge(sem("chunk_done"), n + 1)
                            rope(tile_of(l, name, 0), DK, kr, "kr_ready")
                        elif name[:2] == "uq":
                            dve.wait_ge(sem("chunk_done"), n + 1)
                            rope(tile_of(l, name, 1), P, qr[:, int(name[2]), :], "qr_ready")
                        elif name[:4] == "conv":
                            i = int(name[4])
                            settle()
                            dve.wait_ge(sem("cc_ready"), 4 * l + i + 1)
                            tell(dve.tensor_tensor(u[:, 1:T + 1], tile_of(l, name, 1), ccs[:, :], ALU.mult), "u_ready")
                            own("u_ready")
                            tell(dve.tensor_scalar(cv[:, 0, :], u[:, 0:T], p(l, C_CW + i), None, ALU.mult), "tap")
                            own("tap")
                            tell(dve.scalar_tensor_tensor(cv[:, 1, :], u[:, 1:T + 1], p(l, C_CW + 4 + i),
                                                          cv[:, 0, :], ALU.mult, ALU.add), "tap")
                            own("tap")
                            tell(dve.scalar_tensor_tensor(cv[:, 0, :], u[:, 2:T + 2], p(l, C_CW + 8 + i),
                                                          cv[:, 1, :], ALU.mult, ALU.add), "tap")
                            own("tap")
                            tell(dve.tensor_tensor(o[:, 12 + i, :], tile_of(l, name, 2), cv[:, 0, :], ALU.mult),
                                 "o_conv")
                        elif name[:3] == "out":
                            i = int(name[3])
                            settle()
                            for j in range(4):
                                t = 4 * i + j
                                if j == 0:
                                    dve.wait_ge(sem("half_done"), 4 * l + i + 1)
                                if j == 2:
                                    dve.wait_ge(sem("chunk_done"), n + 1)
                                tell(dve.scalar_tensor_tensor(x[:, t, :], tile_of(l, name, j), acol[:, l, 32 + t:33 + t],
                                                              x[:, t, :], ALU.mult, ALU.add), "x_ready")
                    if c == LAT_AT:
                        invert(A_LAYER * l + N_LAT, 4)
                    if c == LAT_AT + 1:
                        spread(A_LAYER * l + N_LAT)
                        for i in range(5):
                            half = (i // 3) * T
                            gain = p(l, C_QG + i) if i < 3 else p(l, C_KVG + i - 3)
                            tell(dve.scalar_tensor_tensor(lat[:, i, :], lat[:, i, :], gain,
                                                          pn[:, half:half + T], ALU.mult, ALU.mult),
                                 "latn_ready")
                        for i in range(5):
                            dve.wait_ge(sem("lathi_ready"), 5 * l + i + 1)
                            tell(dve.tensor_tensor(lat_lo[:, i, :], lat[:, i, :], lat_hi[:, i, :],
                                                   ALU.subtract), "latlo_ready")
                    h = c - MLA_AT
                    if 0 <= h < HEADS:
                        settle()
                        dve.wait_ge(sem("score_ready"), HEADS * l + h + 1)
                        tell(dve.tensor_reduce(mx[:, :], ps[:, :].rearrange("p (a b) -> p a b", a=2), AX.X,
                                               ALU.max), "mx_ready")
                        own("mx_ready")
                        tell(dve.tensor_scalar(nmx[:, :], mx[:, :], -SM_SCALE, None, ALU.mult), "nmx_ready")
                        dve.wait_ge(sem("exp_ready"), 2 * (HEADS * l + h) + 2)
                        tell(dve.reciprocal(rsi[:, :], rsum[:, :]), "rsi_ready")
                        own("rsi_ready")
                        for q in range(2):
                            tell(dve.tensor_scalar(prob[:, q, :], prob[:, q, :], rsi[:, q:q + 1], None, ALU.mult),
                                 "probn_ready")
                    if c == GATES_AT:
                        settle()
                        dve.wait_ge(sem("gate_psum"), l + 1)
                        for pr in range(PAIRS):
                            for d in range(2):
                                tell(dve.tensor_scalar(cs[:, 2 * pr + d, :], (ps, pt, pn)[pr][:, d * T:(d + 1) * T],
                                                       p(l, (C_BGF, C_BGB)[d] + pr), None, ALU.add), "gx_ready")
                    if c == GATES_AT + 1:
                        settle()
                        dve.wait_ge(sem("ln_ready"), l + 1)
                        every = cs[:, :, :].rearrange("p a b -> p (a b)")
                        tell(dve.scalar_tensor_tensor(every, every, 0.0, gt, ALU.min, ALU.subtract), "la_ready")
                    for pr in range(PAIRS):
                        if c == SCAN_AT + GLA_STEPS * pr - 2 * (pr > 0):
                            settle()
                            scan = kst[:, K_SCAN:K_SCAN + T]
                            fwd, bwd = cs[:, 2 * pr, :], cs[:, 2 * pr + 1, ::-1]
                            tell(dve.tensor_tensor_scan(fwd, scan, fwd, 0.0, ALU.mult, ALU.add), "cs_ready")
                            tell(dve.tensor_tensor_scan(bwd, scan, bwd, 0.0, ALU.mult, ALU.add), "cs_ready")
                    for pr in range(PAIRS):
                        s0 = GLA_AT + GLA_STEPS * pr
                        m = PAIRS * l + pr
                        if c == s0:
                            settle()
                            if m:
                                dve.wait_ge(sem("keT_psum"), m)
                            for d in range(2):
                                b = cs[:, 2 * pr + d, :].rearrange("p (n s) -> p n s", n=NCH)
                                end = b[:, :, CH - 1:CH] if d == 0 else b[:, :, 0:1]
                                tell(dve.tensor_tensor(e_e[:, d, :].rearrange("p (n s) -> p n s", n=NCH),
                                                       end.to_broadcast([P, NCH, CH]), b, ALU.subtract),
                                     "bdiff_ready")
                        if c == s0 + 1:
                            settle()
                            dve.wait_ge(sem("expb_ready"), 2 * m + 2)
                            for d in range(2):
                                b = e_q[:, d, :].rearrange("p (n s) -> p n s", n=NCH)
                                end = b[:, :, CH - 1] if d == 0 else b[:, :, 0]
                                tell(dve.tensor_copy(dec[:, d, :], end), "dec_ready")
                            own("dec_ready")
                            for d in range(2):
                                tell(dve.scalar_tensor_tensor(e_q[:, d, :], o[:, 2 * pr, :], DK ** -0.5,
                                                              e_q[:, d, :], ALU.mult, ALU.mult), "qdec_ready")
                        if c == s0 + 2:
                            settle()
                            if m:
                                dve.wait_ge(sem("pair_done"), m)
                            for d, mask in enumerate((K_MF, K_MB)):
                                if d:
                                    settle()
                                for hh in range(2):
                                    dve.wait_ge(sem("gscore_ready"), 2 * m + hh + 1)
                                    tell(dve.copy_predicated(
                                        st[:, hh, :, :].rearrange("p a b -> p (a b)"),
                                        kst[:, mask:mask + T].bitcast(I32),
                                        (ps, pt)[hh][:, d * T:(d + 1) * T]), "st_ready")
                        if c == s0 + 4:
                            settle()
                            dve.wait_ge(sem("kv_done"), m + 1)
                            even = lambda i: ps[:, i * P:(i + 1) * P]
                            odd = lambda i: pt[:, i * P:(i + 1) * P]
                            tell(dve.tensor_copy(sta[:, 0, 0, :], even(0)), "sta_ready")
                            tell(dve.tensor_copy(sta[:, 1, 0, :], odd(1)), "sta_ready")
                            own("sta_ready")
                            tell(dve.scalar_tensor_tensor(sta[:, 0, 1, :], sta[:, 0, 0, :], dec[:, 0, 1:2],
                                                          odd(0), ALU.mult, ALU.add), "sta_ready")
                            tell(dve.scalar_tensor_tensor(sta[:, 1, 1, :], sta[:, 1, 0, :], dec[:, 1, 2:3],
                                                          even(2), ALU.mult, ALU.add), "sta_ready")
                            own("sta_ready")
                            tell(dve.scalar_tensor_tensor(sta[:, 0, 2, :], sta[:, 0, 1, :], dec[:, 0, 2:3],
                                                          even(1), ALU.mult, ALU.add), "sta_ready")
                            tell(dve.scalar_tensor_tensor(sta[:, 1, 2, :], sta[:, 1, 1, :], dec[:, 1, 1:2],
                                                          odd(2), ALU.mult, ALU.add), "sta_ready")
                    for pr in range(PAIRS):
                        if c == GLAN_AT + pr:
                            invert(A_LAYER * l + N_GLA + pr, 4)
                        if c == GLAN_AT + pr + 1:
                            spread(A_LAYER * l + N_GLA + pr)
                            two = o[:, 2 * pr:2 * pr + 2, :].rearrange("p a b -> p (a b)")
                            tell(dve.scalar_tensor_tensor(two, two, p(l, C_GLAG), (pt, ps, pt)[pr][:, :], ALU.mult, ALU.mult),
                                 "onorm_gla")
                    if c == CONVN_AT:
                        invert(A_LAYER * l + N_CONV, 2)
                    if c == CONVN_AT + 1:
                        spread(A_LAYER * l + N_CONV)
                        for i in range(4):
                            tell(dve.scalar_tensor_tensor(o[:, 12 + i, :], o[:, 12 + i, :], p(l, C_CG + i),
                                                          pn[:, 0:T], ALU.mult, ALU.mult), "onorm_conv")
                    if c == MLAN_AT:
                        invert(A_LAYER * l + N_MLA, 2)
                    if c == MLAN_AT + 1:
                        spread(A_LAYER * l + N_MLA)
                        for i in range(6):
                            tell(dve.scalar_tensor_tensor(o[:, 6 + i, :], o[:, 6 + i, :], p(l, C_MLAG + i),
                                                          pn[:, 0:T], ALU.mult, ALU.mult), "onorm_mla")
                    part = c - FIRST_CHUNK["z3"] - 1
                    for q in ([part, 3] if part == 2 else [part] if 0 <= part < 2 else []):
                        for t in (4 * q, 4 * q + 2):
                            dve.wait_ge(sem("yhi_ready"), 8 * l + t // 2 + 1)
                            tell(dve.tensor_tensor(a_lo[:, t:t + 2, :], o[:, Y_ORDER[t]:Y_ORDER[t] + 2, :],
                                                   a_hi[:, t:t + 2, :], ALU.subtract), "ylo_ready")
                    for n in ada_chunks(l, c):
                        if BY[ADA[n][0]] == "dve":
                            ada_sum(n)
                    if h_due(l, c):
                        ada_bias(bundles_ended(l, c)[0])
                        h_part(l, c // 4 + 1)
                invert(A_LAYER * (l + 1), 2)
            spread(A_LAYER * DEPTH)
            for q in range(4):
                four = slice(4 * q, 4 * q + 4)
                dve.wait_ge(sem("gained"), 4 * q + 4)
                tell(dve.tensor_tensor(o[:, four, :], o[:, four, :],
                                       ps[:, 0:T].unsqueeze(1).to_broadcast([P, 4, T]), ALU.mult), "final_ready")


def pack_stream(w_in, w_out, w_uq, w_ukv):
    import numpy as np
    at = np.cumsum([0, 384, 384, 768, 32, 384, 256, 64, 512, 512, 512, 2048])
    gq, gk, gv, lr, mq, mkv, mkr, cb, cc, cx, z = (np.arange(a, b) for a, b in zip(at[:-1], at[1:]))
    small_tile = -np.ones(P, int)
    small_tile[0:64], small_tile[64:80], small_tile[96:112] = mkr, lr[0:16], lr[16:32]
    head = lambda h, w: np.arange(w * h, w * (h + 1))
    cols = {"latq": np.concatenate([small_tile, mq]), "latkv": mkv, "gq": gq, "gk": gk}
    for i in range(3):
        a, b = head(2 * i, 192), head(2 * i + 1, 192)
        cols[f"uq{i}"] = np.concatenate([a[:128], a[128:], b[128:], b[:128]])
    for i in range(2):
        cols[f"kn{i}"] = np.concatenate([head(h, 256)[:128] for h in range(3 * i, 3 * i + 3)])
        cols[f"vm{i}"] = np.concatenate([head(h, 256)[128:] for h in range(3 * i, 3 * i + 3)])
        cols[f"gv{i}"] = gv[384 * i:384 * i + 384]
    for i in range(CONVT):
        s = slice(P * i, P * i + P)
        cols[f"conv{i}"] = np.concatenate([cc[s], cx[s], cb[s]])
    for i in range(4):
        cols[f"z{i}"] = np.concatenate([z[P * t:P * t + P] for t in Y_ORDER[4 * i:4 * i + 4]])
        cols[f"out{i}"] = np.arange(512 * i, 512 * i + 512)
    y_rows = np.concatenate([np.arange(P * t, P * t + P) for t in Y_ORDER])
    out = np.zeros((DEPTH, STREAM_AT[-1]), w_in.dtype)
    for l in range(DEPTH):
        for c, (g, k) in enumerate(CHUNKS):
            name, width, kt, _ = GROUPS[g]
            src = w_uq[l] if name[:2] == "uq" else w_ukv[l] if name[:2] in ("kn", "vm") else \
                w_out[l][y_rows] if name[:3] == "out" else w_in[l]
            rows = src[k * kt * P:(k + 1) * kt * P]
            part = np.where(cols[name] >= 0, rows[:, np.maximum(cols[name], 0)], np.zeros((), w_in.dtype))
            out[l, STREAM_AT[c]:STREAM_AT[c + 1]] = part.reshape(kt, P, width).transpose(1, 0, 2).ravel()
    return out


def kernel(**inputs):
    import numpy as np
    import concourse.bacc as _bacc
    from concourse import mybir as _mybir
    from concourse.bass_utils import run_bass_kernel_spmd as _run

    a = {k: np.asarray(v) for k, v in inputs.items()}
    f4 = np.float32

    def tiles(v):
        return np.swapaxes(v.reshape(*v.shape[:-1], -1, P), -1, -2)

    par = np.zeros((P, DEPTH, SMALL), f4)
    put = lambda col, v: par.__setitem__((slice(None), slice(None), slice(col, col + v.shape[-1])),
                                         np.moveaxis(v, 0, 1))
    put(C_NORM, tiles(a["norm_g"]))
    put(C_ADAB, tiles(a["ada_b"]))
    put(C_BGF, tiles(a["gla_bg_f"]))
    put(C_BGB, tiles(a["gla_bg_b"]))
    put(C_GLAG, tiles(a["gla_norm_g"]))
    put(C_QG, tiles(a["mla_q_norm_g"]))
    put(C_KVG, tiles(a["mla_kv_norm_g"]))
    put(C_MLAG, tiles(a["mla_out_g"]))
    for tap in range(3):
        put(C_CW + 4 * tap, tiles(a["conv_w"][:, tap]))
    put(C_CG, tiles(a["conv_out_g"]))
    wg = np.zeros((64, DEPTH, 2 * QL), f4)
    wg[0:RANK, :, 0:QL] = a["gla_wg_f"].transpose(1, 0, 2)
    wg[32:32 + RANK, :, QL:] = a["gla_wg_b"].transpose(1, 0, 2)

    const = np.zeros((P, CONST), f4)
    const[:, K_ONES:K_ONES + P] = 1
    const[:, K_ID:K_ID + P] = np.eye(P)
    j, i = np.arange(P)[:, None], np.arange(T)[None, :] % P
    same = j // CH == i // CH
    const[:, K_MF:K_MF + T] = same & (j <= i)
    const[:, K_MB:K_MB + T] = same & (j > i)
    const[:, K_SCAN:K_SCAN + T] = np.arange(T) % CH != 0
    const[:, K_SEL:K_SEL + 4] = np.arange(P)[:, None] % 32 == np.arange(4)
    const[:, K_SIGN] = np.where(np.arange(P) % 64 < 32, 1, -1)
    const[:, K_FREQ] = np.float32(10000.0) ** (-(np.arange(P) % 32).astype(f4) * 2 / np.float32(64))
    const[:, K_EPS] = EPS

    ada = a["ada_w"].reshape(DEPTH, 4, ROWS, P, ADA_GROUPS, WIDE).transpose(0, 4, 1, 3, 2, 5)
    arrays = {
        "xT": np.ascontiguousarray(a["x"][0].T.reshape(KT, P, T).transpose(1, 0, 2)),
        "cT": np.ascontiguousarray(tiles(a["c"][0])),
        "posr": np.ascontiguousarray(a["positions"]),
        "wstream": pack_stream(a["w_in"], a["w_out"], a["mla_w_uq"], a["mla_w_ukv"]),
        "adastream": np.ascontiguousarray(ada).reshape(DEPTH, ADA_GROUPS, 4, P, ROWS * WIDE),
        "wg": wg, "small": par, "finalg": np.ascontiguousarray(tiles(a["final_g"])), "const": const,
    }
    nc = _bacc.Bacc("TRN2", target_bir_lowering=False, num_devices=1,
                     dynamic_dma_scratch_size=1024)
    aps = {n: nc.dram_tensor(n, v.shape, _mybir.dt.from_np(v.dtype), kind="ExternalInput").ap()
           for n, v in arrays.items()}
    out = nc.dram_tensor("out", (P, KT, T), _mybir.dt.float32, kind="ExternalOutput").ap()
    build(nc, out=out, **aps)
    r = _run(nc, [arrays], core_ids=[0]).results[0]["out"]
    return np.ascontiguousarray(r.transpose(1, 0, 2).reshape(D, T).T)[None]
```
